# Optimizing a Trainium2 kernel written in Bass

```python
import math
import jax, jax.numpy as jnp
from jax import lax
import numpy as np

D_MODEL = 1024
BATCH = 1
SEQ = 256
DEPTH = 2

N_MIXERS = 2
N_META = 16
D_FF = 2816
CONV_WIDTH = 3
HEAD_DIM = 64
V_DIM = 2 * HEAD_DIM
N_HEADS = D_MODEL // (2 * HEAD_DIM)
ROT_DIM = HEAD_DIM // 4
ROPE_THETA = 500000.0
Q_BLOCK = 128
FRONT_PAD = Q_BLOCK - N_META
N_CONV_LAYERS = (DEPTH + N_MIXERS - 1) // N_MIXERS
N_ATTN_LAYERS = DEPTH // N_MIXERS
NORM_EPS = 1e-6
SUBLN_EPS = 1e-5
NEG_INF = -1e30


def rms_norm(t, g, eps=NORM_EPS):
    t32 = t.astype(jnp.float32)
    t32 = t32 * lax.rsqrt(jnp.mean(t32 * t32, axis=-1, keepdims=True) + eps)
    return t32.astype(t.dtype) * g.astype(t.dtype)

def swiglu(h, w_gu, w_down):
    g, u = jnp.split(h @ w_gu, 2, axis=-1)
    return (jax.nn.silu(g) * u) @ w_down

def short_conv_mixer(h, w_in, conv_w, w_out):
    b, c, xt = jnp.split(h @ w_in, 3, axis=-1)
    u = c * xt
    u = lax.conv_general_dilated(
        u, conv_w[:, None, :].astype(u.dtype),
        window_strides=(1,), padding=((CONV_WIDTH - 1, 0),),
        dimension_numbers=('NWC', 'WIO', 'NWC'),
        feature_group_count=u.shape[-1])
    return (b * u) @ w_out

def partial_rope(t, cos, sin):
    half = ROT_DIM // 2
    t1 = t[..., :half]
    t2 = t[..., half:ROT_DIM]
    c = cos[None, :, None, None, :]
    s = sin[None, :, None, None, :]
    return jnp.concatenate([t1 * c - t2 * s, t1 * s + t2 * c, t[..., ROT_DIM:]], axis=-1)

def diff_attention_mixer(h, w_qkv, lam_p, subln_g, w_o, lambda_init):
    bsz, seq_len, d = h.shape
    dt = h.dtype
    q, k, v = jnp.split(h @ w_qkv, 3, axis=-1)
    q = q.reshape(bsz, seq_len, N_HEADS, 2, HEAD_DIM)
    k = k.reshape(bsz, seq_len, N_HEADS, 2, HEAD_DIM)
    v = v.reshape(bsz, seq_len, N_HEADS, V_DIM)
    pos = jnp.arange(seq_len, dtype=jnp.float32)
    inv_freq = ROPE_THETA ** (-jnp.arange(0, ROT_DIM, 2, dtype=jnp.float32) / ROT_DIM)
    ang = pos[:, None] * inv_freq[None, :]
    cos = jnp.cos(ang).astype(dt)
    sin = jnp.sin(ang).astype(dt)
    q = partial_rope(q, cos, sin)
    k = partial_rope(k, cos, sin)
    q = jnp.pad(q, ((0, 0), (FRONT_PAD, 0), (0, 0), (0, 0), (0, 0))).transpose(0, 2, 3, 1, 4)
    k = jnp.pad(k, ((0, 0), (FRONT_PAD, 0), (0, 0), (0, 0), (0, 0))).transpose(0, 2, 3, 1, 4)
    v = jnp.pad(v, ((0, 0), (FRONT_PAD, 0), (0, 0), (0, 0))).transpose(0, 2, 1, 3)
    lp = seq_len + FRONT_PAD
    lam32 = lam_p.astype(jnp.float32)
    lam = (jnp.exp(jnp.sum(lam32[0] * lam32[1])) - jnp.exp(jnp.sum(lam32[2] * lam32[3]))
           + lambda_init)
    scale = HEAD_DIM ** -0.5
    outs = []
    for j in range(lp // Q_BLOCK):
        q0, q1 = j * Q_BLOCK, (j + 1) * Q_BLOCK
        qb = q[:, :, :, q0:q1]
        kb = k[:, :, :, :q1]
        vb = v[:, :, :q1]
        s = jnp.einsum('bhcqd,bhckd->bhcqk', qb, kb).astype(jnp.float32) * scale
        qi = jnp.arange(q0, q1)[:, None]
        ki = jnp.arange(q1)[None, :]
        mask = (ki <= qi) & (ki >= FRONT_PAD)
        p = jax.nn.softmax(jnp.where(mask, s, NEG_INF), axis=-1)
        a = p[:, :, 0] - lam * p[:, :, 1]
        outs.append(jnp.einsum('bhqk,bhkv->bhqv', a.astype(dt), vb))
    o = jnp.concatenate(outs, axis=2)[:, :, FRONT_PAD:]
    o = rms_norm(o, subln_g, SUBLN_EPS) * (1.0 - lambda_init)
    o = o.transpose(0, 2, 1, 3).reshape(bsz, seq_len, d)
    return o @ w_o

def first_inputs(seed: int = 0) -> dict:
    key = jax.random.key(seed)
    ks = jax.random.split(key, 20)

    def nrm(k, shape, scale):
        return jax.random.normal(k, shape, jnp.float32) * scale

    def gains(k, shape):
        return 1.0 + nrm(k, shape, 0.02)

    D = D_MODEL
    return {
        'x': nrm(ks[0], (BATCH, SEQ, D), 1.0),
        'meta_tokens': nrm(ks[1], (N_META, D), 1.0),
        'ln_ffn1': gains(ks[2], (DEPTH, 2, D)),
        'ffn1_w_gu': nrm(ks[3], (DEPTH, D, 2 * D_FF), D ** -0.5),
        'ffn1_w_down': nrm(ks[4], (DEPTH, D_FF, D), D_FF ** -0.5),
        'ln_mix': gains(ks[5], (DEPTH, 2, D)),
        'conv_w_in': nrm(ks[6], (N_CONV_LAYERS, D, 3 * D), D ** -0.5),
        'conv_w': nrm(ks[7], (N_CONV_LAYERS, CONV_WIDTH, D), CONV_WIDTH ** -0.5),
        'conv_w_out': nrm(ks[8], (N_CONV_LAYERS, D, D), D ** -0.5),
        'attn_w_qkv': nrm(ks[9], (N_ATTN_LAYERS, D, 3 * D), D ** -0.5),
        'attn_lambda': nrm(ks[10], (N_ATTN_LAYERS, 4, HEAD_DIM), 0.1),
        'attn_subln_g': gains(ks[11], (N_ATTN_LAYERS, V_DIM)),
        'attn_w_o': nrm(ks[12], (N_ATTN_LAYERS, D, D), D ** -0.5),
        'ln_ffn2': gains(ks[13], (DEPTH, 2, D)),
        'ffn2_w_gu': nrm(ks[14], (DEPTH, D, 2 * D_FF), D ** -0.5),
        'ffn2_w_down': nrm(ks[15], (DEPTH, D_FF, D), D_FF ** -0.5),
    }

def first_block(x, meta_tokens, ln_ffn1, ffn1_w_gu, ffn1_w_down, ln_mix,
              conv_w_in, conv_w, conv_w_out, attn_w_qkv, attn_lambda,
              attn_subln_g, attn_w_o, ln_ffn2, ffn2_w_gu, ffn2_w_down):
    bsz = x.shape[0]
    meta = jnp.broadcast_to(meta_tokens.astype(x.dtype)[None], (bsz, N_META, x.shape[-1]))
    h = jnp.concatenate([meta, x], axis=1)
    for i in range(DEPTH):
        f = swiglu(rms_norm(h, ln_ffn1[i, 0]), ffn1_w_gu[i], ffn1_w_down[i])
        h = h + 0.5 * rms_norm(f, ln_ffn1[i, 1])
        hn = rms_norm(h, ln_mix[i, 0])
        j = i // N_MIXERS
        if i % N_MIXERS == 0:
            m = short_conv_mixer(hn, conv_w_in[j], conv_w[j], conv_w_out[j])
        else:
            lambda_init = 0.8 - 0.6 * math.exp(-0.3 * i)
            m = diff_attention_mixer(hn, attn_w_qkv[j], attn_lambda[j],
                                     attn_subln_g[j], attn_w_o[j], lambda_init)
        h = h + rms_norm(m, ln_mix[i, 1])
        f = swiglu(rms_norm(h, ln_ffn2[i, 0]), ffn2_w_gu[i], ffn2_w_down[i])
        h = h + 0.5 * rms_norm(f, ln_ffn2[i, 1])
    return h[:, N_META:]


HGRN_HEADS = 4
HGRN_KEY = 128
HGRN_VAL = 128
HGRN_KW = HGRN_HEADS * HGRN_KEY
HGRN_VW = HGRN_HEADS * HGRN_VAL
HGRN_CHUNK = 64
POOL_WINDOWS = (2, 4, 8, 16)
POOL_GROUP = 128
POOL_WIDTH = POOL_GROUP * len(POOL_WINDOWS)
FOX_HEADS = 16
FOX_HEAD_DIM = 64
FOX_WIDTH = FOX_HEADS * FOX_HEAD_DIM
FOX_BLOCK = 128
EVEN_IN = 2 * HGRN_KW + 2 * HGRN_VW + 2 * POOL_WIDTH
EVEN_MIX = HGRN_VW + POOL_WIDTH
ODD_IN = 4 * FOX_WIDTH + FOX_HEADS
N_EVEN = (DEPTH + 1) // 2
N_ODD = DEPTH // 2
EPS = 1e-6


def rms_norm_2(x, g):
    xf = x.astype(jnp.float32)
    y = xf * lax.rsqrt(jnp.mean(xf * xf, axis=-1, keepdims=True) + EPS)
    return (y * g.astype(jnp.float32)).astype(x.dtype)

def hgrn2_chunked(q, k, v, logf):
    b_, s_, h_, kd = q.shape
    vd = v.shape[-1]
    nc = s_ // HGRN_CHUNK

    def to_chunks(t):
        return t.reshape(b_, nc, HGRN_CHUNK, h_, t.shape[-1]).transpose(1, 0, 3, 2, 4)

    causal = jnp.tril(jnp.ones((HGRN_CHUNK, HGRN_CHUNK), dtype=bool))

    def step(state, inp):
        qc, kc, vc, gc = inp
        cum = jnp.cumsum(gc, axis=2)
        diff = cum[:, :, :, None, :] - cum[:, :, None, :, :]
        decay = jnp.where(causal[:, :, None], jnp.exp(jnp.minimum(diff, 0.0)), 0.0)
        scores = jnp.einsum('bhtk,bhsk,bhtsk->bhts', qc, kc, decay)
        out = (jnp.einsum('bhts,bhsv->bhtv', scores, vc)
               + jnp.einsum('bhtk,bhkv->bhtv', qc * jnp.exp(cum), state))
        last = cum[:, :, -1:, :]
        state = (jnp.exp(last[:, :, 0, :])[..., None] * state
                 + jnp.einsum('bhsk,bhsv->bhkv', kc * jnp.exp(last - cum), vc))
        return state, out

    s0 = jnp.zeros((b_, h_, kd, vd), jnp.float32)
    _, out = lax.scan(step, s0, (to_chunks(q), to_chunks(k), to_chunks(v), to_chunks(logf)))
    return out.transpose(1, 0, 3, 2, 4).reshape(b_, s_, h_, vd)

def multiscale_pool(u):
    b_, s_, _ = u.shape
    groups = u.reshape(b_, s_, len(POOL_WINDOWS), POOL_GROUP)
    csum = jnp.cumsum(groups, axis=1)
    csum = jnp.concatenate([jnp.zeros_like(csum[:, :1]), csum], axis=1)
    pos = jnp.arange(s_)
    outs = []
    for gi, w in enumerate(POOL_WINDOWS):
        cg = csum[:, :, gi]
        lagged = jnp.concatenate([jnp.zeros((b_, w - 1, POOL_GROUP), cg.dtype), cg[:, :s_ - w + 1]], axis=1)
        count = jnp.minimum(pos + 1, w).astype(cg.dtype)[None, :, None]
        outs.append((cg[:, 1:] - lagged) / count - groups[:, :, gi])
    return jnp.stack(outs, axis=2)

def even_mixer(h, w_in, lower, onorm_g, pool_w, pool_scale, w_out):
    b_, s_, _ = h.shape
    proj = (h @ w_in).astype(jnp.float32)
    cuts = [HGRN_KW, 2 * HGRN_KW, 2 * HGRN_KW + HGRN_VW, 2 * HGRN_KW + 2 * HGRN_VW,
            2 * HGRN_KW + 2 * HGRN_VW + POOL_WIDTH]
    q, f, i, g_a, u, g_b = jnp.split(proj, cuts, axis=-1)
    lb = lower.astype(jnp.float32)
    forget = lb + (1.0 - lb) * jax.nn.sigmoid(f)
    logf = jnp.log(forget)
    key = 1.0 - forget
    kh = lambda t: t.reshape(b_, s_, HGRN_HEADS, HGRN_KEY)
    o_a = hgrn2_chunked(kh(q), kh(key), i.reshape(b_, s_, HGRN_HEADS, HGRN_VAL), kh(logf))
    o_a = rms_norm_2(o_a, onorm_g.reshape(HGRN_HEADS, HGRN_VAL)).reshape(b_, s_, HGRN_VW) * jax.nn.silu(g_a)
    pooled = multiscale_pool(u)
    o_b = jnp.einsum('bsgc,gcd->bsgd', pooled, pool_w.astype(jnp.float32)).reshape(b_, s_, POOL_WIDTH)
    o_b = o_b * pool_scale.astype(jnp.float32) * jax.nn.silu(g_b)
    mixed = jnp.concatenate([o_a, o_b], axis=-1).astype(h.dtype)
    return mixed @ w_out

def odd_mixer(h, w_in, b_f, qnorm_g, knorm_g, w_out):
    b_, s_, _ = h.shape
    proj = (h @ w_in).astype(jnp.float32)
    q, k, v, g, fl = jnp.split(proj, [FOX_WIDTH, 2 * FOX_WIDTH, 3 * FOX_WIDTH, 4 * FOX_WIDTH], axis=-1)
    hd = lambda t: t.reshape(b_, s_, FOX_HEADS, FOX_HEAD_DIM)
    q = rms_norm_2(hd(q), qnorm_g).transpose(0, 2, 1, 3)
    k = rms_norm_2(hd(k), knorm_g).transpose(0, 2, 1, 3)
    v = hd(v).transpose(0, 2, 1, 3)
    logf = jax.nn.log_sigmoid(fl + b_f.astype(jnp.float32))
    cumf = jnp.cumsum(logf, axis=1).transpose(0, 2, 1)
    scale = FOX_HEAD_DIM ** -0.5
    outs = []
    for blk in range(s_ // FOX_BLOCK):
        q0 = blk * FOX_BLOCK
        q1 = q0 + FOX_BLOCK
        logits = (jnp.einsum('bhqd,bhkd->bhqk', q[:, :, q0:q1], k[:, :, :q1]) * scale
                  + cumf[:, :, q0:q1, None] - cumf[:, :, None, :q1])
        mask = jnp.arange(q0, q1)[:, None] >= jnp.arange(q1)[None, :]
        probs = jax.nn.softmax(jnp.where(mask, logits, -jnp.inf), axis=-1)
        outs.append(jnp.einsum('bhqk,bhkd->bhqd', probs, v[:, :, :q1]))
    o = jnp.concatenate(outs, axis=2).transpose(0, 2, 1, 3).reshape(b_, s_, FOX_WIDTH)
    o = o * jax.nn.silu(g)
    return o.astype(h.dtype) @ w_out

def second_inputs(seed: int = 0) -> dict:
    key = jax.random.key(seed)
    ks = jax.random.split(key, 16)
    nrm = jax.random.normal
    f32 = jnp.float32
    return {
        'x': nrm(ks[0], (BATCH, SEQ, D_MODEL), f32),
        'c': nrm(ks[1], (BATCH, D_MODEL), f32),
        'norm_g': 1.0 + 0.05 * nrm(ks[2], (DEPTH, D_MODEL), f32),
        'ada_w': 0.5 * D_MODEL ** -0.5 * nrm(ks[3], (DEPTH, D_MODEL, 3 * D_MODEL), f32),
        'ada_b': 0.02 * nrm(ks[4], (DEPTH, 3 * D_MODEL), f32),
        'hgrn_lb': 0.1 * nrm(ks[5], (DEPTH + 1, HGRN_KW), f32),
        'even_w_in': D_MODEL ** -0.5 * nrm(ks[6], (N_EVEN, D_MODEL, EVEN_IN), f32),
        'hgrn_onorm_g': 1.0 + 0.05 * nrm(ks[7], (N_EVEN, HGRN_VW), f32),
        'pool_w': POOL_GROUP ** -0.5 * nrm(ks[8], (N_EVEN, len(POOL_WINDOWS), POOL_GROUP, POOL_GROUP), f32),
        'pool_scale': 1.0 + 0.05 * nrm(ks[9], (N_EVEN, POOL_WIDTH), f32),
        'even_w_out': EVEN_MIX ** -0.5 * nrm(ks[10], (N_EVEN, EVEN_MIX, D_MODEL), f32),
        'odd_w_in': D_MODEL ** -0.5 * nrm(ks[11], (N_ODD, D_MODEL, ODD_IN), f32),
        'fox_b_f': jax.random.uniform(ks[12], (N_ODD, FOX_HEADS), f32, 1.0, 4.0),
        'fox_qnorm_g': 1.0 + 0.05 * nrm(ks[13], (N_ODD, FOX_HEAD_DIM), f32),
        'fox_knorm_g': 1.0 + 0.05 * nrm(ks[14], (N_ODD, FOX_HEAD_DIM), f32),
        'odd_w_out': FOX_WIDTH ** -0.5 * nrm(ks[15], (N_ODD, FOX_WIDTH, D_MODEL), f32),
    }

def second_block(x, c, norm_g, ada_w, ada_b, hgrn_lb, even_w_in, hgrn_onorm_g, pool_w, pool_scale,
              even_w_out, odd_w_in, fox_b_f, fox_qnorm_g, fox_knorm_g, odd_w_out):
    lower = jnp.cumsum(jax.nn.softmax(hgrn_lb.astype(jnp.float32), axis=0), axis=0)
    cond = jax.nn.silu(c)
    for l in range(DEPTH):
        mod = cond @ ada_w[l] + ada_b[l]
        shift, scale, gate = jnp.split(mod, 3, axis=-1)
        h = rms_norm_2(x, norm_g[l]) * (1.0 + scale[:, None, :]) + shift[:, None, :]
        j = l // 2
        if l % 2 == 0:
            y = even_mixer(h, even_w_in[j], lower[l], hgrn_onorm_g[j], pool_w[j], pool_scale[j], even_w_out[j])
        else:
            y = odd_mixer(h, odd_w_in[j], fox_b_f[j], fox_qnorm_g[j], fox_knorm_g[j], odd_w_out[j])
        x = x + gate[:, None, :] * y
    return x


def setup_inputs(seed=0):
    out = dict(first_inputs(seed))
    for name, value in second_inputs(seed + 1).items():
        if name != "x":
            out[name + "_2"] = value
    return out


def reference(
    x, meta_tokens, ln_ffn1, ffn1_w_gu, ffn1_w_down, ln_mix, conv_w_in, conv_w, conv_w_out,
    attn_w_qkv, attn_lambda, attn_subln_g, attn_w_o, ln_ffn2, ffn2_w_gu, ffn2_w_down, c_2,
    norm_g_2, ada_w_2, ada_b_2, hgrn_lb_2, even_w_in_2, hgrn_onorm_g_2, pool_w_2, pool_scale_2,
    even_w_out_2, odd_w_in_2, fox_b_f_2, fox_qnorm_g_2, fox_knorm_g_2, odd_w_out_2,
):
    x = first_block(
        x, meta_tokens, ln_ffn1, ffn1_w_gu, ffn1_w_down, ln_mix, conv_w_in, conv_w, conv_w_out,
        attn_w_qkv, attn_lambda, attn_subln_g, attn_w_o, ln_ffn2, ffn2_w_gu, ffn2_w_down,
    )
    return second_block(
        x, c_2, norm_g_2, ada_w_2, ada_b_2, hgrn_lb_2, even_w_in_2, hgrn_onorm_g_2, pool_w_2,
        pool_scale_2, even_w_out_2, odd_w_in_2, fox_b_f_2, fox_qnorm_g_2, fox_knorm_g_2,
        odd_w_out_2,
    )


_drawn_inputs = setup_inputs


def setup_inputs(seed=0):
    import zlib

    import numpy as np

    out = dict(_drawn_inputs(seed))
    spreads = {}
    factors = {'attn_subln_g': 4.893,
     'ln_ffn2': 3.231,
     'norm_g_2': 5.641,
     'ada_b_2': 5.787,
     'hgrn_lb_2': 8.0,
     'hgrn_onorm_g_2': 8.0,
     'pool_scale_2': 8.0,
     'fox_b_f_2': 4.202,
     'fox_qnorm_g_2': 8.0,
     'fox_knorm_g_2': 8.0}
    for name, (base, spread) in spreads.items():
        noise = np.random.default_rng([zlib.crc32(name.encode()), seed]).standard_normal(out[name].shape)
        drawn = base * np.exp(spread * noise) if base else spread * noise
        out[name] = __import__('jax').numpy.asarray(drawn.astype(out[name].dtype))
    for name, factor in factors.items():
        out[name] = (out[name] * factor).astype(out[name].dtype)
    return out
```

```python
import numpy as np
import concourse.bass as bass
from concourse import mybir
from contextlib import ExitStack

F32 = mybir.dt.float32
F32R = mybir.dt.float32r
I32 = mybir.dt.int32
ALU = mybir.AluOpType
ACT = mybir.ActivationFunctionType
AX = mybir.AxisListType

P = 128
D = 1024
DC = D // P
META = 16
SEQ = 256
T = META + SEQ
FF = 2816
FC = FF // P
HALF = FC // 2
W8, W11 = DC * P, HALF * P
SLOTS = 4
HEADS = 8
LEVELS = 7
LAMBDA_INIT = 0.8 - 0.6 * float(np.exp(-0.3))
NEG = -1e30

STAGES = [("gu0", 11), ("dn0", 4), ("cin", 6), ("cout", 2), ("gu1", 11), ("dn1", 4),
          ("gu2", 11), ("dn2", 4), ("ain", 6), ("aout", 2), ("gu3", 11), ("dn3", 4),
          ("ein", 6), ("eout", 2), ("oin", 8), ("oout", 2)]
QUADS = dict(STAGES)
FIRST_QUAD = {}
_q = 0
for _name, _n in STAGES:
    FIRST_QUAD[_name] = _q
    _q += _n
ALL_QUADS = _q


def wide(stage):
    return stage.startswith("dn")


def unit_base(stage):
    at = 0
    for name, n in STAGES:
        if name == stage:
            return at
        if wide(name) == wide(stage):
            at += SLOTS * n
    return at


def stage_after(stage):
    names = [n for n, _ in STAGES]
    i = names.index(stage) + 1
    return names[i] if i < len(names) else None


PARAMS, _n = {}, 0
for _name, _count in [("ln_ffn1", 32), ("ln_mix", 32), ("ln_ffn2", 32), ("conv_w", 24), ("subln_g", 1),
                      ("lam", 4), ("c", 8), ("norm_g", 16), ("ada_b", 48), ("hgrn_lb", 12), ("onorm_g", 4),
                      ("pool_scale", 4), ("qnorm_g", 1), ("knorm_g", 1), ("b_f", 1)]:
    PARAMS[_name] = (_n, _count)
    _n += _count
N_PARAMS = _n

CONSTS, _n = {}, 0
for _name, _count in [("ident", P), ("ropeswap", P), ("causal", P), ("ones64", P), ("cos", T), ("sin", T),
                      ("pick", 16), ("invcount", 4 * 16)]:
    CONSTS[_name] = (_n, _count)
    _n += _count
N_CONSTS = _n


class Steps:

    def __init__(self, sem):
        self.sem, self.total, self.phases, self.now = sem, 0, {}, {}

    def phase(self, name, steps, times=1):
        self.phases[name] = (self.total, steps, times)
        self.total += len(steps) * times

    def at(self, phase, step, i=0):
        base, steps, _ = self.phases[phase]
        return base + len(steps) * i + steps.index(step) + 1

    def step(self, phase, step):
        _, steps, _ = self.phases[phase]
        k = self.now.get(phase, 0)
        assert steps[k % len(steps)] == step, (phase, step, steps[k % len(steps)])
        self.now[phase] = k + 1
        return self.sem


def build(nc, w8, w11, ada_w, params_in, consts_in, masks_in, pool_w, fl_w, x_in, out, stop=None):
    ctx = ExitStack()
    with ctx:
        def sb(name, shape, dt=F32):
            return ctx.enter_context(nc.sbuf_tensor(name, shape, dt))

        def sem(name):
            return ctx.enter_context(nc.semaphore(name))

        raw = sb("raw", [P, SLOTS, W11])
        w_hi = sb("w_hi", [P, SLOTS, W11], F32R)
        w_lo = sb("w_lo", [P, SLOTS, W11], F32R)
        ada_raw = sb("ada_raw", [P, DC, P])
        h = sb("h", [P, DC, T])
        x_hi = sb("x_hi", [P, DC, T], F32R)
        x_lo = sb("x_lo", [P, DC, T], F32R)
        a_hi = sb("a_hi", [P, FC, T], F32R)
        a_lo = sb("a_lo", [P, FC, T], F32R)
        arena = sb("arena", [P, 32 * T])
        f = arena[:, 24 * T:32 * T].rearrange("p (c t) -> p c t", c=DC)
        xt = sb("xt", [P, 2, T])
        silu_t = sb("silu_t", [P, 2, T])
        sq = sb("sq", [P, 2, T])
        sq_sum = sb("sq_sum", [P, T])
        ln_t = sb("ln_t", [P, 512])
        r_t = sb("r_t", [P, 512])
        prm = sb("prm", [P, N_PARAMS])
        cst = sb("cst", [P, N_CONSTS])
        lvl_mask = sb("lvl_mask", [P, LEVELS, 64], I32)
        poolw = sb("poolw", [P, 4, P])
        flw = sb("flw", [P, DC, 16])
        flw_hi = sb("flw_hi", [P, DC, 16], F32R)
        flw_lo = sb("flw_lo", [P, DC, 16], F32R)
        ones = sb("ones", [P, P])
        eps6 = sb("eps6", [P, 1])
        eps5 = sb("eps5", [P, 1])
        one = sb("one", [P, 1])
        half_g = sb("half_g", [P, 4, DC])
        sub_g = sb("sub_g", [P, 1])
        gq = sb("gq", [P, 1])
        lam_pair = sb("lam_pair", [P, 2])
        lam_exp = sb("lam_exp", [P, 2])
        neg_lam = sb("neg_lam", [P, 1])
        cond = sb("cond", [P, DC])
        mod = sb("mod", [P, 2, 3, DC])
        gs = sb("gs", [P, 2, DC])
        lb = sb("lb", [P, 2, 4])
        lb3 = sb("lb3", [P, 3, 4])
        lbm = sb("lbm", [P, 4])
        work = sb("work", [P, 4, T])
        qs, ks, vs = (work[:, i, :] for i in range(3))
        q_half = sb("q_half", [P, 2, T])
        vn = sb("vn", [P, 3, P])
        small = sb("small", [P, 32])
        at2 = sb("at2", [META, META])
        pool_a = ada_raw[:, :, :].rearrange("p a b -> p (a b)").rearrange("p (g t) -> p g t", g=4)
        pool_b = work[:, :, 0:SEQ]
        lnb = poolw[0:16, :, :].rearrange("p a b -> p (a b)").rearrange("p (e k) -> p e k", e=2)

        bank = [ctx.enter_context(nc.psum_tensor(f"bank{i}", [P, 512], F32)) for i in range(8)]
        STAT, ADA = bank[4], bank[5]

        raw_in = [sem(f"raw_in{s}") for s in range(SLOTS)]
        w_hi_ready, w_lo_ready, unit_done = sem("w_hi_ready"), sem("w_lo_ready"), sem("unit_done")
        ada_in, setup_in, out_done = sem("ada_in"), sem("setup_in"), sem("out_done")
        act, vec, pe, pool = (Steps(sem(n)) for n in ("scalar_steps", "vector_steps", "tensor_steps", "gpsimd_steps"))

        def par(name, i=0, n=1):
            a = PARAMS[name][0] + i
            return prm[:, a:a + n]

        def con(name):
            a, n = CONSTS[name]
            return cst[:, a:a + n]

        ident = con("ident")
        CH = [str(c) for c in range(DC)]

        def lagged(first, second, n=DC):
            out_ = []
            for c in range(n + 1):
                if c < n:
                    out_.append((first, c))
                if c:
                    out_.append((second, c - 1))
            return out_

        def names(pairs):
            return [a + str(c) for a, c in pairs]

        pool.phase("setup", ["ones", "eps6", "eps5", "one", "q_half"])
        vec.phase("setup", ["lam", "half0", "half1", "half2", "half3", "subg", "gq", "lbm", "lb0", "lb1", "lb2",
                            "lbs", "lbt", "lbr", "lbq", "lbn", "lamd", "laml"])
        act.phase("setup", ["cond", "lame", "lbe"])
        pe.phase("setup", ["lams"])
        PRES = ["pre0", "prec", "pre1", "pre2", "prea", "pre3", "pree", "preo"]

        def declare_pre(n):
            act.phase(n, names([("sq", c) for c in range(DC)]) + ["ln", "r"] + names([("hi", c) for c in range(DC)]))
            pe.phase(n, names([("ss", c) for c in range(DC)]))
            vec.phase(n, (["gs"] if n in ("pree", "preo") else []) + names(lagged("t", "lo")))

        def declare_res(n):
            pe.phase(n, ["ss"])
            act.phase(n, ["ln", "r"])
            vec.phase(n, names(lagged("t", "h")))

        def declare_ffn(k):
            declare_pre(f"pre{k}")
            g, d = f"gu{k}", f"dn{k}"
            act.phase(g, ["silu0", "silu1"], 11)
            vec.phase(g, ["hi0", "full0", "lo0", "hi1", "full1", "lo1"], 11)
            pe.phase(g, ["ada"], 11)
            act.phase(d, ["f0", "sq0", "f1", "sq1"], 4)
            pool.phase(d, ["zero"])
            pool.phase(d + "s", ["add0", "add1"], 3)
            pool.phase(d + "t", ["add0"])
            pe.phase(d, ["ada"])
            vec.phase(d, ["mod"])
            declare_res(f"res{k}")

        def declare_out1(n, res):
            act.phase(n, ["f0", "sq0", "f1", "sq1", "f2", "sq2", "f3", "sq3"], 2)
            pool.phase(n, ["zero"] + [f"add{o}" for o in range(7)])
            declare_res(res)

        declare_ffn(0)
        declare_pre("prec")
        act.phase("cin", ["e0", "e1", "e2", "e3"], 6)
        vec.phase("conv", ["u"] + ["w2" + c for c in CH] + ["w1" + c for c in CH] + ["w0" + c for c in CH]
                  + ["hi", "full", "lo"])
        declare_out1("cout", "resc")
        declare_ffn(1)
        declare_ffn(2)
        declare_pre("prea")
        act.phase("ain", ["e0", "e1", "e2", "e3"], 6)
        pe.phase("att", ["pq", "pk", "vt", "s0", "s1", "s2", "s3", "t0", "t1", "t2", "o", "oss"], HEADS)
        vec.phase("att", ["qc", "kc", "qx", "kx", "qs0", "qs1", "ks", "m0", "n0", "m1", "n1", "m2", "m3", "n2",
                          "r0", "l0", "b0", "a0", "r1", "l1", "b1", "a1", "r2", "l2", "b2", "a2",
                          "hi", "full", "lo"], HEADS)
        act.phase("att", ["vs", "vn", "vn2", "e00", "e01", "e10", "e11", "e20", "e21", "at0", "at1", "at2", "at3",
                          "osq", "ln", "r"], HEADS)
        declare_out1("aout", "resa")
        declare_ffn(3)
        declare_pre("pree")
        act.phase("ein", ["e0", "e1", "e2", "e3"], 6)
        act.phase("hg", ["sig", "sga", "sgb", "vn0", "vn1", "s2"] + [f"{a}{i}" for i in range(4) for a in ("sq", "ln", "r")])
        lv = []
        for i in range(LEVELS):
            lv += [f"cp{i}", f"qp{i}", f"kp{i}", f"tp{i}"]
        vec.phase("hg", ["fg0", "fg1", "fg2", "fg3", "key", "fm", "q0", "dg0", "dg1"] + lv
                  + [f"{a}{i}" for i in range(4) for a in ("on", "hi", "full", "lo")]
                  + [f"{a}{i}" for i in range(4, 8) for a in ("on", "hi", "full", "lo")])
        pe.phase("hg", ["vt0", "vt1", "dg"] + [f"lv{i}" for i in range(LEVELS + 1)] + ["pv0", "pv1", "pv2", "pv3"]
                 + [f"ss{i}" for i in range(4)] + [f"pl{i}" for i in range(4)])
        pl = []
        for lvl in range(4):
            pl += [f"c{lvl}", f"s{lvl}"]
        pool.phase("hg", pl + [f"i{g}" for g in range(4)] + [f"j{g}" for g in range(4)] + [f"p{g}" for g in range(4)])
        vec.phase("eout", ["h0", "h1", "h2", "h3"], 2)
        declare_pre("preo")
        act.phase("oin", ["e0", "e1", "e2", "e3"], 8)
        act.phase("fl", ["whi", "cp0", "cp1", "exp", "ln", "sg"])
        vec.phase("fl", ["wlo", "z", "nz", "az", "logf", "cum", "ncum"])
        pe.phase("fl", ["fl", "tr"])
        act.phase("fox", ["sqq", "sqk", "vs", "ln", "r", "vn", "e00", "e01", "e10", "e11", "pt0", "pt1"], 8)
        vec.phase("fox", ["qn0", "qn1", "kn", "d0", "d1", "m0", "n0", "m1", "n1", "r0", "p00", "p01", "r1", "p10", "p11",
                          "hi", "full", "lo"], 8)
        pe.phase("fox", ["nq", "nk", "vt", "s0", "s1", "t0", "t1", "o"], 8)
        vec.phase("oout", ["h0", "h1", "h2", "h3"], 2)

        H_READY = {"pre0": None, "prec": ("res0", "h"), "pre1": ("resc", "h"), "pre2": ("res1", "h"),
                   "prea": ("res2", "h"), "pre3": ("resa", "h"), "pree": ("res3", "h"), "preo": ("eout", None)}
        GAIN = {"pre0": ("ln_ffn1", 0), "res0": ("half", 0), "prec": ("ln_mix", 0), "resc": ("ln_mix", 8),
                "pre1": ("ln_ffn2", 0), "res1": ("half", 1), "pre2": ("ln_ffn1", 16), "res2": ("half", 2),
                "prea": ("ln_mix", 16), "resa": ("ln_mix", 24), "pre3": ("ln_ffn2", 16), "res3": ("half", 3)}

        def gain(phase, c):
            name, first = GAIN[phase]
            return half_g[:, first, c:c + 1] if name == "half" else par(name, first + c)

        def tok(phase):
            return slice(META, T) if phase in ("pree", "preo") else slice(0, T)

        IN_PRE = {"gu0": "pre0", "cin": "prec", "gu1": "pre1", "gu2": "pre2", "ain": "prea", "gu3": "pre3",
                  "ein": "pree", "oin": "preo"}

        block = ctx.enter_context(nc.Block())

        @block.sync
        def _(sp):
            sp.dma_start(prm[:, :], params_in).then_inc(setup_in, 16)
            sp.dma_start(h[:, :, :], x_in).then_inc(setup_in, 16)
            sp.dma_start(cst[:, :], consts_in).then_inc(setup_in, 16)
            sp.dma_start(lvl_mask[:, :, :], masks_in).then_inc(setup_in, 16)
            sp.dma_start(poolw[:, :, :], pool_w).then_inc(setup_in, 16)
            sp.dma_start(flw[:, :, :], fl_w).then_inc(setup_in, 16)

            def load(stage, i):
                src, n = (w11, W11) if wide(stage) else (w8, W8)
                q = FIRST_QUAD[stage] + i
                for s in range(SLOTS):
                    if not (isinstance(i, int) and q == 0):
                        sp.wait_ge(w_lo_ready, SLOTS * q - SLOTS + s + 1)
                    sp.dma_start(raw[:, s, 0:n],
                                 src[bass.ds(unit_base(stage) + SLOTS * i + s, 1), :, :].rearrange("a p n -> (a p) n")
                                 ).then_inc(raw_in[s], 16)

            def load_ada(k, i):
                if isinstance(i, int) and i == 11:
                    sp.wait_ge(pe.sem, pe.at(f"gu{k}", "ada", 10))
                elif isinstance(i, int) and i == 0:
                    if k:
                        sp.wait_ge(pe.sem, pe.at(f"dn{k - 1}", "ada"))
                else:
                    sp.wait_ge(pe.sem, pe.at(f"gu{k}", "ada", i - 1))
                sp.dma_start(ada_raw[:, :, :], ada_w[bass.ds(12 * k + i, 1), :, :, :].rearrange("a p k n -> (a p) k n")
                             ).then_inc(ada_in, 16)

            for stage, n in STAGES:
                k = int(stage[-1]) if stage[:2] in ("gu", "dn") else None
                load(stage, 0)
                if stop and stage == stage_after(stop):
                    break
                if stage[:2] == "gu":
                    load_ada(k, 0)
                if stage[:2] == "dn":
                    load_ada(k, 11)
                with sp.Fori(1, n) as i:
                    load(stage, i)
                    if stage[:2] == "gu":
                        load_ada(k, i)
            sp.wait_ge(vec.sem, vec.total if stop is None else
                       vec.at(*{"dn0": ("res0", "h7"), "cout": ("resc", "h7"), "aout": ("resa", "h7"),
                                "dn3": ("res3", "h7"), "eout": ("eout", "h3", 1)}[stop]))
            sp.dma_start(out, h[:, :, META:T]).then_inc(out_done, 16)
            sp.wait_ge(out_done, 16)

        @block.scalar
        def _(sc):
            def split_hi(stage, i, s):
                n = W11 if wide(stage) else W8
                q = FIRST_QUAD[stage] + i
                sc.wait_ge(raw_in[s], 16 * q + 16)
                if not (isinstance(i, int) and q == 0):
                    sc.wait_ge(unit_done, SLOTS * q - SLOTS + s + 1)
                sc.activation(w_hi[:, s, 0:n], raw[:, s, 0:n], ACT.Copy).then_inc(w_hi_ready, 1)

            def split_next(stage, i, s):
                if isinstance(i, int) and i == QUADS[stage] - 1:
                    nxt = stage_after(stage)
                    if nxt:
                        split_hi(nxt, 0, s)
                else:
                    split_hi(stage, i + 1, s)

            def quads(stage, body):
                body(0)
                if QUADS[stage] > 2:
                    with sc.Fori(1, QUADS[stage] - 1) as i:
                        body(i)
                body(QUADS[stage] - 1)

            def rsqrt(phase, src, n, scale, eps, ready):
                sc.wait_ge(*ready)
                sc.activation(ln_t[:, 0:n], src, ACT.Ln, bias=eps[:, :], scale=scale).then_inc(act.step(phase, "ln"), 1)
                sc.wait_ge(act.sem, act.at(phase, "ln"))
                sc.activation(r_t[:, 0:n], ln_t[:, 0:n], ACT.Exp, scale=-0.5).then_inc(act.step(phase, "r"), 1)

            def pre(phase):
                ts = tok(phase)
                n = ts.stop - ts.start
                for c in range(DC):
                    src = H_READY[phase]
                    if src and src[0] == "eout":
                        sc.wait_ge(vec.sem, vec.at("eout", f"h{c % 4}", c // 4))
                    elif src:
                        sc.wait_ge(vec.sem, vec.at(src[0], f"h{c}"))
                    if c >= 2:
                        sc.wait_ge(pe.sem, pe.at(phase, f"ss{c - 2}"))
                    sc.activation(sq[:, c % 2, 0:n], h[:, c, ts], ACT.Square).then_inc(act.step(phase, f"sq{c}"), 1)
                rsqrt(phase, STAT[:, 0:n], n, 1.0 / D, eps6, (pe.sem, pe.at(phase, "ss7")))
                for c in range(DC):
                    sc.wait_ge(vec.sem, vec.at(phase, f"t{c}"))
                    if n == T:
                        sc.activation(x_hi[:, c, 0:n], xt[:, c % 2, 0:n], ACT.Copy).then_inc(act.step(phase, f"hi{c}"), 1)
                    else:
                        l = 0 if phase == "pree" else 1
                        sc.activation(x_hi[:, c, 0:n], xt[:, c % 2, 0:n], ACT.Identity, bias=mod[:, l, 0, c:c + 1]
                                      ).then_inc(act.step(phase, f"hi{c}"), 1)

            def ffn(k):
                g, d = f"gu{k}", f"dn{k}"
                pre(f"pre{k}")

                def gu_quad(i):
                    q = FIRST_QUAD[g] + i
                    for p in range(2):
                        sc.wait_ge(unit_done, SLOTS * q + 2 * p + 1)
                        sc.wait_ge(vec.sem, vec.at(g, f"full{p}", i - 1))
                        sc.activation(silu_t[:, p, :], bank[2 * p][:, 0:T], ACT.Silu).then_inc(act.step(g, f"silu{p}"), 1)
                        split_next(g, i, 2 * p)
                        split_next(g, i, 2 * p + 1)

                quads(g, gu_quad)

                def dn_quad(i):
                    q = FIRST_QUAD[d] + i
                    for p in range(2):
                        o = 2 * i + p
                        split_next(d, i, 2 * p)
                        sc.wait_ge(unit_done, SLOTS * q + 2 * p + 2)
                        sc.activation(f[:, bass.ds(o, 1), :].rearrange("p a t -> p (a t)"), bank[2 * p][:, 0:T],
                                      ACT.Copy).then_inc(act.step(d, f"f{p}"), 1)
                        if not isinstance(i, int) or i > 0:
                            sc.wait_ge(pool.sem, pool.at(d + "s", f"add{p}", i - 1))
                        sc.activation(sq[:, p, :], bank[2 * p][:, 0:T], ACT.Square).then_inc(act.step(d, f"sq{p}"), 1)
                        split_next(d, i, 2 * p + 1)

                quads(d, dn_quad)
                rsqrt(f"res{k}", STAT[:, 0:T], T, 1.0 / D, eps6, (pe.sem, pe.at(f"res{k}", "ss")))

            def evacuate(stage, n):
                def quad(i):
                    q = FIRST_QUAD[stage] + i
                    for s in range(SLOTS):
                        sc.wait_ge(unit_done, SLOTS * q + s + 1)
                        sc.activation(arena[:, bass.ds((SLOTS * i + s) * n, n)], bank[s][:, 0:n], ACT.Copy
                                      ).then_inc(act.step(stage, f"e{s}"), 1)
                        split_next(stage, i, s)
                quads(stage, quad)

            def out1(stage, res):
                for i in range(2):
                    q = FIRST_QUAD[stage] + i
                    for s in range(SLOTS):
                        o = SLOTS * i + s
                        sc.wait_ge(unit_done, SLOTS * q + s + 1)
                        sc.activation(f[:, o, :], bank[s][:, 0:T], ACT.Copy).then_inc(act.step(stage, f"f{s}"), 1)
                        if o >= 2:
                            sc.wait_ge(pool.sem, pool.at(stage, f"add{o - 2}"))
                        sc.activation(sq[:, o % 2, :], bank[s][:, 0:T], ACT.Square).then_inc(act.step(stage, f"sq{s}"), 1)
                        split_next(stage, i, s)
                rsqrt(res, STAT[:, 0:T], T, 1.0 / D, eps6, (pe.sem, pe.at(res, "ss")))

            sc.wait_ge(setup_in, 96)
            sc.activation(cond[:, :], par("c", 0, DC), ACT.Silu).then_inc(act.step("setup", "cond"), 1)
            sc.wait_ge(pe.sem, pe.at("setup", "lams"))
            sc.activation(lam_exp[:, :], bank[7][:, 0:2], ACT.Exp).then_inc(act.step("setup", "lame"), 1)
            sc.wait_ge(vec.sem, vec.at("setup", "lb2"))
            sc.activation(lb3[:, :, :], lb3[:, :, :], ACT.Exp).then_inc(act.step("setup", "lbe"), 1)
            sc.wait_ge(pool.sem, pool.at("setup", "one"))
            for s in range(SLOTS):
                split_hi("gu0", 0, s)

            ffn(0)
            if stop == "dn0": return
            pre("prec")
            evacuate("cin", T)
            out1("cout", "resc")
            if stop == "cout": return
            ffn(1)
            ffn(2)
            pre("prea")
            evacuate("ain", T)

            with sc.Fori(0, HEADS) as hd:
                sc.wait_ge(pe.sem, pe.at("att", "vt", hd - 1))
                sc.wait_ge(act.sem, act.at("ain", "e3", 5))
                sc.activation(vs[:, :], arena[:, bass.ds((16 + hd) * T, T)], ACT.Copy).then_inc(act.step("att", "vs"), 1)
                sc.wait_ge(pe.sem, pe.at("att", "vt", hd))
                sc.activation(vn[:, 0:2, :].rearrange("p a v -> p (a v)"), bank[2][:, 0:256], ACT.Copy
                              ).then_inc(act.step("att", "vn"), 1)
                sc.activation(vn[0:META, 2, :], bank[2][0:META, 256:384], ACT.Copy).then_inc(act.step("att", "vn2"), 1)
                for qb in range(3):
                    n_q = P if qb < 2 else META
                    n_k = P * (qb + 1) if qb < 2 else T
                    sc.wait_ge(vec.sem, vec.at("att", f"n{qb}", hd))
                    sc.wait_ge(pe.sem, pe.at("att", f"t{qb}", hd - 1))
                    for c in range(2):
                        src = (bank[4][:, c * P:(c + 1) * P], bank[5][:, c * 256:(c + 1) * 256],
                               bank[6 + c][:, 0:T])[qb]
                        sc.activation(f[0:n_q, 2 * qb + c, 0:n_k], src[0:n_q, :], ACT.Exp, scale=0.125,
                                      bias=small[0:n_q, 8 + 2 * qb + c:9 + 2 * qb + c],
                                      accum_out=small[0:n_q, 16 + 2 * qb + c:17 + 2 * qb + c]
                                      ).then_inc(act.step("att", f"e{qb}{c}"), 1)
                at_ = f[:, 6:8, :]
                sc.wait_ge(pe.sem, pe.at("att", "t0", hd))
                sc.activation(at_[:, 0, 0:P], bank[3][:, 0:P], ACT.Copy).then_inc(act.step("att", "at0"), 1)
                sc.wait_ge(pe.sem, pe.at("att", "t1", hd))
                sc.activation(at_[:, 0:2, P:2 * P], bank[4][:, 0:2 * P].rearrange("p (k q) -> p k q", k=2), ACT.Copy
                              ).then_inc(act.step("att", "at1"), 1)
                sc.wait_ge(pe.sem, pe.at("att", "t2", hd))
                sc.activation(at_[:, 0:2, 256:T], bank[0][:, 0:32].rearrange("p (k q) -> p k q", k=2), ACT.Copy
                              ).then_inc(act.step("att", "at2"), 1)
                sc.activation(at2[:, :], bank[0][0:META, 32:48], ACT.Copy).then_inc(act.step("att", "at3"), 1)
                sc.wait_ge(pe.sem, pe.at("att", "o", hd))
                sc.activation(sq[:, 0, :], bank[1][:, 0:T], ACT.Square).then_inc(act.step("att", "osq"), 1)
                sc.wait_ge(pe.sem, pe.at("att", "oss", hd))
                sc.activation(ln_t[:, 0:T], bank[2][:, 0:T], ACT.Ln, bias=eps5[:, :], scale=1.0 / P
                              ).then_inc(act.step("att", "ln"), 1)
                sc.wait_ge(act.sem, act.at("att", "ln", hd))
                sc.wait_ge(vec.sem, vec.at("att", "full", hd - 1))
                sc.activation(r_t[:, 0:T], ln_t[:, 0:T], ACT.Exp, scale=-0.5).then_inc(act.step("att", "r"), 1)
            out1("aout", "resa")
            if stop == "aout": return
            ffn(3)
            if stop == "dn3": return
            pre("pree")
            evacuate("ein", SEQ)

            ar = arena[:, 0:32 * SEQ]
            sc.wait_ge(act.sem, act.at("ein", "e3", 5))
            sc.activation(ar[:, 4 * SEQ:8 * SEQ], ar[:, 4 * SEQ:8 * SEQ], ACT.Sigmoid).then_inc(act.step("hg", "sig"), 1)
            sc.activation(ar[:, 12 * SEQ:16 * SEQ], ar[:, 12 * SEQ:16 * SEQ], ACT.Silu).then_inc(act.step("hg", "sga"), 1)
            sc.activation(ar[:, 20 * SEQ:24 * SEQ], ar[:, 20 * SEQ:24 * SEQ], ACT.Silu).then_inc(act.step("hg", "sgb"), 1)
            i_tok = ar[:, 8 * SEQ:12 * SEQ]
            for j in range(2):
                sc.wait_ge(pe.sem, pe.at("hg", f"vt{j}"))
                if j == 0:
                    sc.wait_ge(pe.sem, pe.at("hg", "vt1"))
                sc.activation(i_tok[:, j * 512:(j + 1) * 512], bank[6 + j][:, :], ACT.Copy).then_inc(act.step("hg", f"vn{j}"), 1)
            sc.wait_ge(pe.sem, pe.at("hg", f"lv{LEVELS}"))
            sc.activation(xt[:, :, 0:256], bank[6][:, :].rearrange("p (a b) -> p a b", a=2), ACT.Copy
                          ).then_inc(act.step("hg", "s2"), 1)
            for i in range(4):
                sc.wait_ge(pe.sem, pe.at("hg", f"pv{i}"))
                if i >= 2:
                    sc.wait_ge(pe.sem, pe.at("hg", f"ss{i - 2}"))
                sc.activation(silu_t[:, i % 2, 0:SEQ], bank[i][:, 0:SEQ], ACT.Square).then_inc(act.step("hg", f"sq{i}"), 1)
                sc.wait_ge(pe.sem, pe.at("hg", f"ss{i}"))
                if i == 0:
                    sc.wait_ge(vec.sem, vec.at("hg", f"tp{LEVELS - 1}"))
                sc.activation(ln_t[:, 0:SEQ], bank[4 + i % 2][:, 0:SEQ], ACT.Ln, bias=eps6[:, :], scale=1.0 / P
                              ).then_inc(act.step("hg", f"ln{i}"), 1)
                sc.wait_ge(act.sem, act.at("hg", f"ln{i}"))
                if i >= 2:
                    sc.wait_ge(vec.sem, vec.at("hg", f"on{i - 2}"))
                sc.activation(r_t[:, (i % 2) * SEQ:(i % 2 + 1) * SEQ], ln_t[:, 0:SEQ], ACT.Exp, scale=-0.5
                              ).then_inc(act.step("hg", f"r{i}"), 1)

            def out2(stage):
                for i in range(2):
                    for s in range(SLOTS):
                        split_next(stage, i, s)

            out2("eout")
            if stop == "eout": return
            pre("preo")
            evacuate("oin", SEQ)

            sc.activation(flw_hi[:, :, :], flw[:, :, :], ACT.Copy).then_inc(act.step("fl", "whi"), 1)
            sc.wait_ge(pe.sem, pe.at("fl", "fl"))
            for j in range(2):
                sc.activation(small[:, 16 * j:16 * j + 16], bank[j][:, 0:16], ACT.Copy).then_inc(act.step("fl", f"cp{j}"), 1)
            sc.wait_ge(vec.sem, vec.at("fl", "az"))
            sc.activation(pool_a[0:16, 3, :], pool_a[0:16, 2, :], ACT.Exp, scale=-1.0).then_inc(act.step("fl", "exp"), 1)
            sc.wait_ge(act.sem, act.at("fl", "exp"))
            sc.activation(pool_b[0:16, 0, :], pool_a[0:16, 3, :], ACT.Ln, bias=one[0:16, :]).then_inc(act.step("fl", "ln"), 1)
            sc.activation(ar[:, 24 * SEQ:32 * SEQ], ar[:, 24 * SEQ:32 * SEQ], ACT.Silu).then_inc(act.step("fl", "sg"), 1)

            with sc.Fori(0, 8) as j:
                sc.wait_ge(pe.sem, pe.at("fox", "nk", j - 1))
                sc.activation(sq[:, 0, 0:SEQ], ar[:, bass.ds(j * SEQ, SEQ)], ACT.Square).then_inc(act.step("fox", "sqq"), 1)
                sc.activation(sq[:, 1, 0:SEQ], ar[:, bass.ds((8 + j) * SEQ, SEQ)], ACT.Square).then_inc(act.step("fox", "sqk"), 1)
                sc.wait_ge(pe.sem, pe.at("fox", "vt", j - 1))
                sc.activation(vs[:, 0:SEQ], ar[:, bass.ds((16 + j) * SEQ, SEQ)], ACT.Copy).then_inc(act.step("fox", "vs"), 1)
                sc.wait_ge(pe.sem, pe.at("fox", "nk", j))
                sc.activation(ln_t[:, :], bank[0][:, :], ACT.Ln, bias=eps6[:, :], scale=1.0 / 64).then_inc(act.step("fox", "ln"), 1)
                sc.wait_ge(act.sem, act.at("fox", "ln", j))
                sc.wait_ge(vec.sem, vec.at("fox", "kn", j - 1))
                sc.activation(r_t[:, :], ln_t[:, :], ACT.Exp, scale=-0.5).then_inc(act.step("fox", "r"), 1)
                sc.wait_ge(pe.sem, pe.at("fox", "vt", j))
                sc.wait_ge(pe.sem, pe.at("fox", "o", j - 1))
                sc.activation(vn[:, 0:2, :].rearrange("p a v -> p (a v)"), bank[2][:, 0:256], ACT.Copy
                              ).then_inc(act.step("fox", "vn"), 1)
                for qb in range(2):
                    n_k = P * (qb + 1)
                    sc.wait_ge(vec.sem, vec.at("fox", f"n{qb}", j))
                    sc.wait_ge(pe.sem, pe.at("fox", f"t{qb}", j - 1))
                    for e in range(2):
                        sc.activation(pool_a[:, 2 * qb + e, 0:n_k], bank[4 + qb][:, e * n_k:(e + 1) * n_k], ACT.Exp,
                                      bias=small[:, 8 + 2 * qb + e:9 + 2 * qb + e],
                                      accum_out=small[:, 16 + 2 * qb + e:17 + 2 * qb + e]
                                      ).then_inc(act.step("fox", f"e{qb}{e}"), 1)
                sc.wait_ge(pe.sem, pe.at("fox", "t0", j))
                sc.activation(xt[:, 0, 0:256], bank[6][:, 0:256], ACT.Copy).then_inc(act.step("fox", "pt0"), 1)
                sc.wait_ge(pe.sem, pe.at("fox", "t1", j))
                sc.activation(silu_t[:, :, 0:256], bank[7][:, :].rearrange("p (a b) -> p a b", a=2), ACT.Copy
                              ).then_inc(act.step("fox", "pt1"), 1)
            out2("oout")

        @block.vector
        def _(ve):
            def split_lo(stage, i, s):
                n = W11 if wide(stage) else W8
                q = FIRST_QUAD[stage] + i
                ve.wait_ge(w_hi_ready, SLOTS * q + s + 1)
                ve.tensor_tensor(w_lo[:, s, 0:n], raw[:, s, 0:n], w_hi[:, s, 0:n].bitcast(F32), ALU.subtract
                                 ).then_inc(w_lo_ready, 1)

            def split_next(stage, i, s):
                if isinstance(i, int) and i == QUADS[stage] - 1:
                    nxt = stage_after(stage)
                    if nxt:
                        split_lo(nxt, 0, s)
                else:
                    split_lo(stage, i + 1, s)

            def quads(stage, body):
                body(0)
                if QUADS[stage] > 2:
                    with ve.Fori(1, QUADS[stage] - 1) as i:
                        body(i)
                body(QUADS[stage] - 1)

            def own(phase, step, i=0):
                ve.wait_ge(vec.sem, vec.at(phase, step, i))

            def pre(phase):
                ts = tok(phase)
                n = ts.stop - ts.start
                l = {"pree": 0, "preo": 1}.get(phase)
                if l is not None:
                    ve.scalar_tensor_tensor(gs[:, l, :], mod[:, l, 1, :], 1.0, par("norm_g", 8 * l, 8), ALU.add, ALU.mult
                                            ).then_inc(vec.step(phase, "gs"), 1)
                    own(phase, "gs")
                ve.wait_ge(act.sem, act.at(phase, "r"))
                for what, c in lagged("t", "lo"):
                    if what == "t":
                        if c >= 2:
                            own(phase, f"lo{c - 2}")
                        g = gain(phase, c) if l is None else gs[:, l, c:c + 1]
                        ve.scalar_tensor_tensor(xt[:, c % 2, 0:n], h[:, c, ts], g, r_t[:, 0:n], ALU.mult, ALU.mult
                                                ).then_inc(vec.step(phase, f"t{c}"), 1)
                    else:
                        ve.wait_ge(act.sem, act.at(phase, f"hi{c}"))
                        if l is None:
                            ve.tensor_tensor(x_lo[:, c, 0:n], xt[:, c % 2, 0:n], x_hi[:, c, 0:n].bitcast(F32),
                                             ALU.subtract).then_inc(vec.step(phase, f"lo{c}"), 1)
                        else:
                            ve.scalar_tensor_tensor(x_lo[:, c, 0:n], xt[:, c % 2, 0:n], mod[:, l, 0, c:c + 1],
                                                    x_hi[:, c, 0:n].bitcast(F32), ALU.add, ALU.subtract
                                                    ).then_inc(vec.step(phase, f"lo{c}"), 1)

            def res(phase):
                ve.wait_ge(act.sem, act.at(phase, "r"))
                for what, c in lagged("t", "h"):
                    if what == "t":
                        if c >= 2:
                            own(phase, f"h{c - 2}")
                        ve.tensor_tensor(xt[:, c % 2, :], f[:, c, :], r_t[:, 0:T], ALU.mult
                                         ).then_inc(vec.step(phase, f"t{c}"), 1)
                    else:
                        own(phase, f"t{c}")
                        ve.scalar_tensor_tensor(h[:, c, :], xt[:, c % 2, :], gain(phase, c), h[:, c, :],
                                                ALU.mult, ALU.add).then_inc(vec.step(phase, f"h{c}"), 1)

            def ffn(k):
                g, d = f"gu{k}", f"dn{k}"
                pre(f"pre{k}")

                def gu_quad(i):
                    q = FIRST_QUAD[g] + i
                    for p in range(2):
                        j = 2 * i + p
                        ve.wait_ge(act.sem, act.at(g, f"silu{p}", i))
                        ve.wait_ge(unit_done, SLOTS * q + 2 * p + 2)
                        hi = a_hi[:, bass.ds(j, 1), :].rearrange("p a t -> p (a t)")
                        lo = a_lo[:, bass.ds(j, 1), :].rearrange("p a t -> p (a t)")
                        ve.tensor_tensor(hi, silu_t[:, p, :], bank[2 * p + 1][:, 0:T], ALU.mult
                                         ).then_inc(vec.step(g, f"hi{p}"), 1)
                        own(g, f"lo{p}", i - 1)
                        ve.tensor_tensor(xt[:, p, :], silu_t[:, p, :], bank[2 * p + 1][:, 0:T], ALU.mult
                                         ).then_inc(vec.step(g, f"full{p}"), 1)
                        split_next(g, i, 2 * p)
                        own(g, f"full{p}", i)
                        ve.tensor_tensor(lo, xt[:, p, :], hi.bitcast(F32), ALU.subtract).then_inc(vec.step(g, f"lo{p}"), 1)
                        split_next(g, i, 2 * p + 1)

                quads(g, gu_quad)

                def dn_quad(i):
                    for s in range(SLOTS):
                        split_next(d, i, s)

                quads(d, dn_quad)
                ve.wait_ge(pe.sem, pe.at(d, "ada"))
                flat = mod[:, :, :, :].rearrange("p l a c -> p (l a c)")
                ve.tensor_tensor(flat[:, 12 * k:12 * k + 12], ADA[:, 0:12], par("ada_b", 12 * k, 12), ALU.add
                                 ).then_inc(vec.step(d, "mod"), 1)
                res(f"res{k}")

            def evac_quads(stage):
                def quad(i):
                    for s in range(SLOTS):
                        split_next(stage, i, s)
                quads(stage, quad)

            ve.wait_ge(setup_in, 96)
            lam = PARAMS["lam"][0]
            ve.tensor_tensor(lam_pair[:, :], prm[:, lam:lam + 3:2], prm[:, lam + 1:lam + 4:2], ALU.mult
                             ).then_inc(vec.step("setup", "lam"), 1)
            for k, (name, first) in enumerate([("ln_ffn1", 8), ("ln_ffn2", 8), ("ln_ffn1", 24), ("ln_ffn2", 24)]):
                ve.tensor_scalar(half_g[:, k, :], par(name, first, 8), 0.5, None, ALU.mult
                                 ).then_inc(vec.step("setup", f"half{k}"), 1)
            ve.tensor_scalar(sub_g[:, :], par("subln_g"), 1.0 - LAMBDA_INIT, None, ALU.mult).then_inc(vec.step("setup", "subg"), 1)
            ve.tensor_scalar(gq[:, :], par("qnorm_g"), 0.125, None, ALU.mult).then_inc(vec.step("setup", "gq"), 1)
            row = [par("hgrn_lb", 4 * i, 4) for i in range(3)]
            ve.tensor_tensor(lbm[:, :], row[0], row[1], ALU.max).then_inc(vec.step("setup", "lbm"), 1)
            own("setup", "lbm")
            ve.tensor_tensor(lbm[:, :], lbm[:, :], row[2], ALU.max).then_inc(vec.step("setup", "lb0"), 1)
            own("setup", "lb0")
            ve.tensor_tensor(lb3[:, 0, :], row[0], lbm[:, :], ALU.subtract).then_inc(vec.step("setup", "lb1"), 1)
            ve.tensor_tensor(lb3[:, 1:3, :], prm[:, PARAMS["hgrn_lb"][0] + 4:PARAMS["hgrn_lb"][0] + 12].rearrange("p (r c) -> p r c", r=2),
                             lbm[:, :].unsqueeze(1).broadcast_to([P, 2, 4]), ALU.subtract).then_inc(vec.step("setup", "lb2"), 1)
            ve.wait_ge(act.sem, act.at("setup", "lbe"))
            ve.tensor_tensor(lb[:, 0, :], lb3[:, 0, :], lb3[:, 1, :], ALU.add).then_inc(vec.step("setup", "lbs"), 1)
            own("setup", "lbs")
            ve.tensor_tensor(lb[:, 0, :], lb[:, 0, :], lb3[:, 2, :], ALU.add).then_inc(vec.step("setup", "lbt"), 1)
            own("setup", "lbt")
            ve.reciprocal(lb[:, 1, :], lb[:, 0, :]).then_inc(vec.step("setup", "lbr"), 1)
            own("setup", "lbr")
            ve.tensor_tensor(lb[:, 0, :], lb3[:, 0, :], lb[:, 1, :], ALU.mult).then_inc(vec.step("setup", "lbq"), 1)
            own("setup", "lbq")
            ve.tensor_scalar(lb[:, 1, :], lb[:, 0, :], -1.0, 1.0, ALU.mult, ALU.add).then_inc(vec.step("setup", "lbn"), 1)
            ve.wait_ge(act.sem, act.at("setup", "lame"))
            ve.tensor_tensor(neg_lam[:, :], lam_exp[:, 1:2], lam_exp[:, 0:1], ALU.subtract).then_inc(vec.step("setup", "lamd"), 1)
            own("setup", "lamd")
            ve.tensor_scalar(neg_lam[:, :], neg_lam[:, :], -LAMBDA_INIT, None, ALU.add).then_inc(vec.step("setup", "laml"), 1)
            for s in range(SLOTS):
                split_lo("gu0", 0, s)

            ffn(0)
            if stop == "dn0": return
            pre("prec")
            evac_quads("cin")
            ar = arena[:, 0:24 * T]
            c_, x_, b_ = (ar[:, 8 * i * T:8 * (i + 1) * T].rearrange("p (c t) -> p c t", c=DC) for i in range(3))
            ve.wait_ge(act.sem, act.at("cin", "e3", 5))
            ve.tensor_tensor(x_, c_, x_, ALU.mult).then_inc(vec.step("conv", "u"), 1)
            own("conv", "u")
            for c in range(DC):
                ve.tensor_scalar(c_[:, c, :], x_[:, c, :], par("conv_w", 16 + c), None, ALU.mult
                                 ).then_inc(vec.step("conv", f"w2{c}"), 1)
            for back, c in [(b, c) for b in (1, 2) for c in range(DC)]:
                own("conv", f"w{3 - back}{c}")
                ve.scalar_tensor_tensor(c_[:, c, back:T], x_[:, c, 0:T - back], par("conv_w", 8 * (2 - back) + c),
                                        c_[:, c, back:T], ALU.mult, ALU.add).then_inc(vec.step("conv", f"w{2 - back}{c}"), 1)
            own("conv", "w07")
            ve.tensor_tensor(a_hi[:, 0:DC, :], b_, c_, ALU.mult).then_inc(vec.step("conv", "hi"), 1)
            ve.tensor_tensor(x_, b_, c_, ALU.mult).then_inc(vec.step("conv", "full"), 1)
            own("conv", "full")
            ve.tensor_tensor(a_lo[:, 0:DC, :], x_, a_hi[:, 0:DC, :].bitcast(F32), ALU.subtract).then_inc(vec.step("conv", "lo"), 1)
            evac_quads("cout")
            res("resc")
            if stop == "cout": return
            ffn(1)
            ffn(2)
            pre("prea")
            evac_quads("ain")

            with ve.Fori(0, HEADS) as hd:
                q_ = arena[:, bass.ds(hd * T, T)]
                k_ = arena[:, bass.ds((8 + hd) * T, T)]
                ve.wait_ge(act.sem, act.at("ain", "e3", 5))
                ve.wait_ge(pe.sem, pe.at("att", "s3", hd - 1))
                ve.tensor_tensor(qs[:, :], q_, con("cos"), ALU.mult).then_inc(vec.step("att", "qc"), 1)
                ve.tensor_tensor(ks[:, :], k_, con("cos"), ALU.mult).then_inc(vec.step("att", "kc"), 1)
                ve.wait_ge(pe.sem, pe.at("att", "pq", hd))
                own("att", "ks", hd - 1)
                ve.tensor_tensor(xt[:, 0, :], bank[0][:, 0:T], con("sin"), ALU.mult).then_inc(vec.step("att", "qx"), 1)
                ve.wait_ge(pe.sem, pe.at("att", "pk", hd))
                own("att", "lo", hd - 1)
                ve.tensor_tensor(xt[:, 1, :], bank[1][:, 0:T], con("sin"), ALU.mult).then_inc(vec.step("att", "kx"), 1)
                own("att", "qx", hd)
                for c in range(2):
                    ve.tensor_tensor(q_half[64 * c:64 * c + 64, c, :], qs[64 * c:64 * c + 64, :], xt[64 * c:64 * c + 64, 0, :],
                                     ALU.add).then_inc(vec.step("att", f"qs{c}"), 1)
                own("att", "kx", hd)
                ve.tensor_tensor(ks[:, :], ks[:, :], xt[:, 1, :], ALU.add).then_inc(vec.step("att", "ks"), 1)
                ve.wait_ge(pe.sem, pe.at("att", "s0", hd))
                ve.reduce_max(small[:, 0:2], bank[4][:, 0:256].rearrange("p (c k) -> p c k", c=2), AX.X
                              ).then_inc(vec.step("att", "m0"), 1)
                own("att", "m0", hd)
                ve.tensor_scalar(small[:, 8:10], small[:, 0:2], -0.125, None, ALU.mult).then_inc(vec.step("att", "n0"), 1)
                ve.wait_ge(pe.sem, pe.at("att", "s1", hd))
                ve.reduce_max(small[:, 2:4], bank[5][:, 0:512].rearrange("p (c k) -> p c k", c=2), AX.X
                              ).then_inc(vec.step("att", "m1"), 1)
                own("att", "m1", hd)
                ve.tensor_scalar(small[:, 10:12], small[:, 2:4], -0.125, None, ALU.mult).then_inc(vec.step("att", "n1"), 1)
                for c in range(2):
                    ve.wait_ge(pe.sem, pe.at("att", f"s{2 + c}", hd))
                    ve.reduce_max(small[0:META, 4 + c:5 + c], bank[6 + c][0:META, 0:T], AX.X).then_inc(vec.step("att", f"m{2 + c}"), 1)
                own("att", "m3", hd)
                ve.tensor_scalar(small[0:META, 12:14], small[0:META, 4:6], -0.125, None, ALU.mult).then_inc(vec.step("att", "n2"), 1)
                for qb in range(3):
                    n_q = P if qb < 2 else META
                    n_k = P * (qb + 1) if qb < 2 else T
                    e0, e1 = f[0:n_q, 2 * qb, 0:n_k], f[0:n_q, 2 * qb + 1, 0:n_k]
                    r = small[0:n_q, 24 + 2 * qb:26 + 2 * qb]
                    ve.wait_ge(act.sem, act.at("att", f"e{qb}1", hd))
                    ve.reciprocal(r, small[0:n_q, 16 + 2 * qb:18 + 2 * qb]).then_inc(vec.step("att", f"r{qb}"), 1)
                    own("att", f"r{qb}", hd)
                    ve.tensor_scalar(r[:, 1:2], r[:, 1:2], neg_lam[0:n_q, :], None, ALU.mult).then_inc(vec.step("att", f"l{qb}"), 1)
                    own("att", f"l{qb}", hd)
                    ve.tensor_scalar(e1, e1, r[:, 1:2], None, ALU.mult).then_inc(vec.step("att", f"b{qb}"), 1)
                    own("att", f"b{qb}", hd)
                    ve.scalar_tensor_tensor(e0, e0, r[:, 0:1], e1, ALU.mult, ALU.add).then_inc(vec.step("att", f"a{qb}"), 1)
                hi = a_hi[:, bass.ds(hd, 1), :].rearrange("p a t -> p (a t)")
                lo = a_lo[:, bass.ds(hd, 1), :].rearrange("p a t -> p (a t)")
                ve.wait_ge(act.sem, act.at("att", "r", hd))
                ve.scalar_tensor_tensor(hi, bank[1][:, 0:T], sub_g[:, :], r_t[:, 0:T], ALU.mult, ALU.mult
                                        ).then_inc(vec.step("att", "hi"), 1)
                ve.scalar_tensor_tensor(xt[:, 1, :], bank[1][:, 0:T], sub_g[:, :], r_t[:, 0:T], ALU.mult, ALU.mult
                                        ).then_inc(vec.step("att", "full"), 1)
                own("att", "full", hd)
                ve.tensor_tensor(lo, xt[:, 1, :], hi.bitcast(F32), ALU.subtract).then_inc(vec.step("att", "lo"), 1)
            evac_quads("aout")
            res("resa")
            if stop == "aout": return
            ffn(3)
            if stop == "dn3": return
            pre("pree")
            evac_quads("ein")

            ar2 = arena[:, 0:32 * SEQ]
            q_, f_ = ar2[:, 0:4 * SEQ], ar2[:, 4 * SEQ:8 * SEQ]
            key, qp = ar2[:, 24 * SEQ:28 * SEQ], ar2[:, 28 * SEQ:32 * SEQ]
            st = arena[:, 0:4 * SEQ]
            ve.wait_ge(act.sem, act.at("hg", "sig"))
            for i in range(4):
                ve.tensor_scalar(f_[:, i * SEQ:(i + 1) * SEQ], f_[:, i * SEQ:(i + 1) * SEQ], lb[:, 1, i:i + 1],
                                 lb[:, 0, i:i + 1], ALU.mult, ALU.add).then_inc(vec.step("hg", f"fg{i}"), 1)
            own("hg", "fg3")
            ve.tensor_scalar(key, f_, -1.0, 1.0, ALU.mult, ALU.add).then_inc(vec.step("hg", "key"), 1)
            own("hg", "key")
            ve.tensor_scalar(f_, f_, 1.0, None, ALU.min).then_inc(vec.step("hg", "fm"), 1)
            own("hg", "fm")
            ve.tensor_tensor(qp, q_, f_, ALU.mult).then_inc(vec.step("hg", "q0"), 1)
            ve.wait_ge(pe.sem, pe.at("hg", "dg"))
            own("hg", "q0")
            idb = ident.unsqueeze(1).broadcast_to([P, 4, P])
            for j in range(2):
                ve.tensor_tensor(st[:, j * 512:(j + 1) * 512].rearrange("p (a t) -> p a t", a=4),
                                 bank[j][:, :].rearrange("p (a t) -> p a t", a=4), idb, ALU.mult
                                 ).then_inc(vec.step("hg", f"dg{j}"), 1)
            own("hg", "dg1")
            tot = f_
            tbuf = [ln_t[:, :], sq[:, 0, :]]
            for i in range(LEVELS):
                b = 1 << i
                nb = 64 // b
                ve.wait_ge(pe.sem, pe.at("hg", f"lv{i}"))
                for_all = st.rearrange("p (a n r b) -> p a n r b", a=8, n=nb, r=2, b=b)
                msk = lvl_mask[:, i, :].rearrange("p (n b) -> p n b", n=nb).unsqueeze(1).broadcast_to([P, 8, nb, b])
                ve.copy_predicated(for_all[:, :, :, 1, :], msk,
                                   bank[2 + i % 2][:, :].rearrange("p (a n b) -> p a n b", a=8, n=nb)
                                   ).then_inc(vec.step("hg", f"cp{i}"), 1)
                t3 = tot.rearrange("p (n r) -> p n r", r=2)
                n2 = 1024 // (2 * b)
                qv = qp.rearrange("p (n r b) -> p n r b", r=2, b=b)
                kv = key.rearrange("p (n r b) -> p n r b", r=2, b=b)
                ve.tensor_tensor(qv[:, :, 1, :], qv[:, :, 1, :], t3[:, :, 0].unsqueeze(2).broadcast_to([P, n2, b]), ALU.mult
                                 ).then_inc(vec.step("hg", f"qp{i}"), 1)
                ve.tensor_tensor(kv[:, :, 0, :], kv[:, :, 0, :], t3[:, :, 1].unsqueeze(2).broadcast_to([P, n2, b]), ALU.mult
                                 ).then_inc(vec.step("hg", f"kp{i}"), 1)
                new = tbuf[i % 2][:, 0:n2]
                ve.tensor_tensor(new, t3[:, :, 0], t3[:, :, 1], ALU.mult).then_inc(vec.step("hg", f"tp{i}"), 1)
                own("hg", f"tp{i}")
                tot = new
            sga, sgb = ar2[:, 12 * SEQ:16 * SEQ], ar2[:, 20 * SEQ:24 * SEQ]
            for i in range(8):
                if i < 4:
                    ve.wait_ge(act.sem, act.at("hg", f"r{i}"))
                    src, g, other = bank[i][:, 0:SEQ], par("onorm_g", i), r_t[:, (i % 2) * SEQ:(i % 2 + 1) * SEQ]
                    gate = sga[:, i * SEQ:(i + 1) * SEQ]
                else:
                    ve.wait_ge(pe.sem, pe.at("hg", f"pl{i - 4}"))
                    src, g = bank[6 + i % 2][:, 0:SEQ], par("pool_scale", i - 4)
                    other = gate = sgb[:, (i - 4) * SEQ:(i - 3) * SEQ]
                t0, t1 = (f_[:, (2 * b + i % 2) * SEQ:(2 * b + i % 2 + 1) * SEQ] for b in range(2))
                if i == 0:
                    own("hg", f"tp{LEVELS - 1}")
                if i >= 2:
                    own("hg", f"lo{i - 2}")
                ve.scalar_tensor_tensor(t0, src, g, other, ALU.mult, ALU.mult).then_inc(vec.step("hg", f"on{i}"), 1)
                own("hg", f"on{i}")
                if i < 4:
                    ve.tensor_tensor(a_hi[:, i, 0:SEQ], t0, gate, ALU.mult).then_inc(vec.step("hg", f"hi{i}"), 1)
                    ve.tensor_tensor(t1, t0, gate, ALU.mult).then_inc(vec.step("hg", f"full{i}"), 1)
                else:
                    ve.tensor_copy(a_hi[:, i, 0:SEQ], t0).then_inc(vec.step("hg", f"hi{i}"), 1)
                    ve.tensor_copy(t1, t0).then_inc(vec.step("hg", f"full{i}"), 1)
                own("hg", f"full{i}")
                ve.tensor_tensor(a_lo[:, i, 0:SEQ], t1, a_hi[:, i, 0:SEQ].bitcast(F32), ALU.subtract
                                 ).then_inc(vec.step("hg", f"lo{i}"), 1)

            def out2(stage, l):
                for i in range(2):
                    q = FIRST_QUAD[stage] + i
                    for s in range(SLOTS):
                        split_next(stage, i, s)
                        c = SLOTS * i + s
                        ve.wait_ge(unit_done, SLOTS * q + s + 1)
                        ve.scalar_tensor_tensor(h[:, c, META:T], bank[s][:, 0:SEQ], mod[:, l, 2, c:c + 1],
                                                h[:, c, META:T], ALU.mult, ALU.add).then_inc(vec.step(stage, f"h{s}"), 1)

            out2("eout", 0)
            if stop == "eout": return
            pre("preo")
            evac_quads("oin")

            ve.wait_ge(act.sem, act.at("fl", "whi"))
            ve.tensor_tensor(flw_lo[:, :, :], flw[:, :, :], flw_hi[:, :, :].bitcast(F32), ALU.subtract).then_inc(vec.step("fl", "wlo"), 1)
            z, nz, az = (pool_a[0:16, i, :] for i in range(3))
            ls, cum, ncum = (pool_b[0:16, i, :] for i in (1, 0, 3))
            ve.wait_ge(pe.sem, pe.at("fl", "tr"))
            ve.tensor_scalar(z, bank[2][0:16, 0:SEQ], par("b_f")[0:16, :], None, ALU.add).then_inc(vec.step("fl", "z"), 1)
            own("fl", "z")
            ve.tensor_scalar(nz, z, -1.0, None, ALU.mult).then_inc(vec.step("fl", "nz"), 1)
            own("fl", "nz")
            ve.tensor_tensor(az, z, nz, ALU.max).then_inc(vec.step("fl", "az"), 1)
            ve.wait_ge(act.sem, act.at("fl", "ln"))
            ve.scalar_tensor_tensor(ls, z, 0.0, pool_b[0:16, 0, :], ALU.min, ALU.subtract).then_inc(vec.step("fl", "logf"), 1)
            own("fl", "logf")
            ones2 = ones[0:16, 0:1].broadcast_to([16, SEQ])
            ve.tensor_tensor_scan(cum, ones2, ls, 0.0, ALU.mult, ALU.add
                                  ).then_inc(vec.step("fl", "cum"), 1)
            own("fl", "cum")
            ve.tensor_scalar(ncum, cum, -1.0, None, ALU.mult).then_inc(vec.step("fl", "ncum"), 1)
            own("fl", "ncum")

            with ve.Fori(0, 8) as j:
                ve.wait_ge(act.sem, act.at("fox", "r", j))
                ve.wait_ge(pe.sem, pe.at("fox", "s1", j - 1))
                for e in range(2):
                    ps = slice(64 * e, 64 * e + 64)
                    ve.scalar_tensor_tensor(q_half[ps, e, 0:SEQ], ar2[ps, bass.ds(j * SEQ, SEQ)], gq[ps, :], r_t[ps, 0:SEQ],
                                            ALU.mult, ALU.mult).then_inc(vec.step("fox", f"qn{e}"), 1)
                ve.scalar_tensor_tensor(ks[:, 0:SEQ], ar2[:, bass.ds((8 + j) * SEQ, SEQ)], par("knorm_g"), r_t[:, SEQ:512],
                                        ALU.mult, ALU.mult).then_inc(vec.step("fox", "kn"), 1)
                pick = CONSTS["pick"][0]
                for e in range(2):
                    ve.tensor_scalar(lnb[0:16, e, :], ncum, cst[0:16, bass.ds(pick + 2 * j + e, 1)], None, ALU.mult
                                     ).then_inc(vec.step("fox", f"d{e}"), 1)
                for qb in range(2):
                    n_k = P * (qb + 1)
                    ve.wait_ge(pe.sem, pe.at("fox", f"s{qb}", j))
                    ve.reduce_max(small[:, 2 * qb:2 * qb + 2], bank[4 + qb][:, 0:2 * n_k].rearrange("p (e k) -> p e k", e=2),
                                  AX.X).then_inc(vec.step("fox", f"m{qb}"), 1)
                    own("fox", f"m{qb}", j)
                    ve.tensor_scalar(small[:, 8 + 2 * qb:10 + 2 * qb], small[:, 2 * qb:2 * qb + 2], -1.0, None, ALU.mult
                                     ).then_inc(vec.step("fox", f"n{qb}"), 1)
                for qb in range(2):
                    n_k = P * (qb + 1)
                    ve.wait_ge(act.sem, act.at("fox", f"e{qb}1", j))
                    ve.reciprocal(small[:, 24 + 2 * qb:26 + 2 * qb], small[:, 16 + 2 * qb:18 + 2 * qb]
                                  ).then_inc(vec.step("fox", f"r{qb}"), 1)
                    own("fox", f"r{qb}", j)
                    for e in range(2):
                        ve.tensor_scalar(pool_a[:, 2 * qb + e, 0:n_k], pool_a[:, 2 * qb + e, 0:n_k], small[:, 24 + 2 * qb + e:25 + 2 * qb + e],
                                         None, ALU.mult).then_inc(vec.step("fox", f"p{qb}{e}"), 1)
                hi = a_hi[:, bass.ds(j, 1), 0:SEQ].rearrange("p a t -> p (a t)")
                lo = a_lo[:, bass.ds(j, 1), 0:SEQ].rearrange("p a t -> p (a t)")
                gate = ar2[:, bass.ds((24 + j) * SEQ, SEQ)]
                ve.wait_ge(act.sem, act.at("fl", "sg"))
                ve.wait_ge(pe.sem, pe.at("fox", "o", j))
                ve.tensor_tensor(hi, bank[3][:, 0:SEQ], gate, ALU.mult).then_inc(vec.step("fox", "hi"), 1)
                own("fox", "lo", j - 1)
                ve.tensor_tensor(xt[:, 1, 0:SEQ], bank[3][:, 0:SEQ], gate, ALU.mult).then_inc(vec.step("fox", "full"), 1)
                own("fox", "full", j)
                ve.tensor_tensor(lo, xt[:, 1, 0:SEQ], hi.bitcast(F32), ALU.subtract).then_inc(vec.step("fox", "lo"), 1)
            out2("oout", 1)

        @block.gpsimd
        def _(gp):
            gp.memset(ones[:, :], 1.0).then_inc(pool.step("setup", "ones"), 1)
            gp.memset(eps6[:, :], 1e-6).then_inc(pool.step("setup", "eps6"), 1)
            gp.memset(eps5[:, :], 1e-5).then_inc(pool.step("setup", "eps5"), 1)
            gp.memset(one[:, :], 1.0).then_inc(pool.step("setup", "one"), 1)
            gp.memset(q_half[:, :, :], 0.0).then_inc(pool.step("setup", "q_half"), 1)

            def zero(phase, prev):
                if prev:
                    gp.wait_ge(pe.sem, pe.at(*prev))
                gp.memset(sq_sum[:, :], 0.0).then_inc(pool.step(phase, "zero"), 1)
                gp.wait_ge(pool.sem, pool.at(phase, "zero"))

            def ffn_sums(k, prev):
                d = f"dn{k}"
                zero(d, prev)

                def add(i, p, phase, j):
                    gp.wait_ge(act.sem, act.at(d, f"sq{p}", i))
                    gp.tensor_tensor(sq_sum[:, :], sq_sum[:, :], sq[:, p, :], ALU.add).then_inc(pool.step(phase, f"add{p}"), 1)
                    gp.wait_ge(pool.sem, pool.at(phase, f"add{p}", j))
                with gp.Fori(0, 3) as i:
                    for p in range(2):
                        add(i, p, d + "s", i)
                add(3, 0, d + "t", 0)

            def out1(stage, prev):
                zero(stage, prev)
                for o in range(7):
                    gp.wait_ge(act.sem, act.at(stage, f"sq{o % 4}", o // 4))
                    gp.tensor_tensor(sq_sum[:, :], sq_sum[:, :], sq[:, o % 2, :], ALU.add).then_inc(pool.step(stage, f"add{o}"), 1)
                    gp.wait_ge(pool.sem, pool.at(stage, f"add{o}"))

            ffn_sums(0, None)
            if stop == "dn0": return
            out1("cout", ("res0", "ss"))
            if stop == "cout": return
            ffn_sums(1, ("resc", "ss"))
            ffn_sums(2, ("res1", "ss"))
            out1("aout", ("res2", "ss"))
            if stop == "aout": return
            ffn_sums(3, ("resa", "ss"))
            if stop == "dn3": return

            ar = arena[:, 0:32 * SEQ]
            u = ar[:, 16 * SEQ:20 * SEQ].rearrange("p (g t) -> p g t", g=4)
            bufs = [pool_a[:, :, :], pool_b[:, :, :]]
            gp.wait_ge(act.sem, act.at("ein", "e3", 5))
            src = u
            for lvl in range(4):
                d = 1 << lvl
                dst = bufs[lvl % 2]
                gp.tensor_copy(dst[:, lvl:4, 0:d], src[:, lvl:4, 0:d]).then_inc(pool.step("hg", f"c{lvl}"), 1)
                gp.tensor_tensor(dst[:, lvl:4, d:SEQ], src[:, lvl:4, d:SEQ], src[:, lvl:4, 0:SEQ - d], ALU.add
                                 ).then_inc(pool.step("hg", f"s{lvl}"), 1)
                gp.wait_ge(pool.sem, pool.at("hg", f"s{lvl}"))
                src = dst
            inv = CONSTS["invcount"][0]
            for g in range(4):
                gp.tensor_tensor(bufs[g % 2][:, g, 0:16], bufs[g % 2][:, g, 0:16], cst[:, inv + 16 * g:inv + 16 * g + 16],
                                 ALU.mult).then_inc(pool.step("hg", f"i{g}"), 1)
            for g in range(4):
                gp.tensor_scalar(bufs[g % 2][:, g, 16:SEQ], bufs[g % 2][:, g, 16:SEQ], 1.0 / (2 << g), None, ALU.mult
                                 ).then_inc(pool.step("hg", f"j{g}"), 1)
            gp.wait_ge(pool.sem, pool.at("hg", "j3"))
            for g in range(4):
                gp.tensor_tensor(bufs[g % 2][:, g, :], bufs[g % 2][:, g, :], u[:, g, :], ALU.subtract
                                 ).then_inc(pool.step("hg", f"p{g}"), 1)

        @block.tensor
        def _(te):
            def product(dst, s, w, rhs_hi, rhs_lo, first, last):
                a = w * P
                te.matmul(dst, w_hi[:, s, a:a + P], rhs_hi, start=first, stop=False)
                te.matmul(dst, w_hi[:, s, a:a + P], rhs_lo, start=False, stop=False)
                return te.matmul(dst, w_lo[:, s, a:a + P], rhs_hi, start=False, stop=last)

            def quads(stage, body):
                body(0)
                with te.Fori(1, QUADS[stage]) as i:
                    body(i)

            def project(stage, n, src_hi, src_lo, free, after=None, k_ready=None, extra=None):
                def quad(i):
                    q = FIRST_QUAD[stage] + i
                    for s in range(SLOTS):
                        te.wait_ge(w_lo_ready, SLOTS * q + s + 1)
                        if isinstance(i, int) and i == 0:
                            if s == 0 and after:
                                te.wait_ge(*after)
                        else:
                            te.wait_ge(*free(s, i - 1))
                        for k in range(DC):
                            if isinstance(i, int) and i == 0 and s == 0 and k_ready:
                                te.wait_ge(*k_ready(k))
                            last = product(bank[s][:, 0:n], s, k, src_hi[:, k, 0:n], src_lo[:, k, 0:n],
                                           k == 0, k == DC - 1)
                        last.then_inc(unit_done, 1)
                    if extra:
                        extra(i)
                quads(stage, quad)

            def pre(phase):
                n = tok(phase).stop - tok(phase).start
                for c in range(DC):
                    te.wait_ge(act.sem, act.at(phase, f"sq{c}"))
                    te.matmul(STAT[:, 0:n], ones[:, :], sq[:, c % 2, 0:n], start=(c == 0), stop=(c == DC - 1)
                              ).then_inc(pe.step(phase, f"ss{c}"), 1)

            def lo_ready(phase):
                return lambda k: (vec.sem, vec.at(phase, f"lo{k}"))

            def ada(k, i):
                te.wait_ge(ada_in, 16 * (12 * k + i) + 16)
                if k and isinstance(i, int) and i == 0:
                    te.wait_ge(vec.sem, vec.at(f"dn{k - 1}", "mod"))
                col = ADA[:, bass.ds(i, 1)]
                for kk in range(DC):
                    last = te.matmul(col, ada_raw[:, kk, :], cond[:, kk:kk + 1], start=(kk == 0), stop=(kk == DC - 1))
                return last

            def res(phase, last_add, last_sq):
                te.wait_ge(pool.sem, last_add)
                te.matmul(STAT[:, 0:T], ones[:, :], sq_sum[:, :], start=True, stop=False)
                te.wait_ge(act.sem, last_sq)
                te.matmul(STAT[:, 0:T], ones[:, :], sq[:, 1, :], start=False, stop=True).then_inc(pe.step(phase, "ss"), 1)

            def ffn(k):
                g, d = f"gu{k}", f"dn{k}"
                pre(f"pre{k}")
                project(g, T, x_hi, x_lo, lambda s, i: (vec.sem, vec.at(g, f"full{s // 2}", i)),
                        k_ready=lo_ready(f"pre{k}"),
                        extra=lambda i: ada(k, i).then_inc(pe.step(g, "ada"), 1))

                def dn_quad(i):
                    q = FIRST_QUAD[d] + i
                    for s in range(SLOTS):
                        te.wait_ge(w_lo_ready, SLOTS * q + s + 1)
                        p = s // 2
                        if isinstance(i, int) and i == 0:
                            if s == 0:
                                te.wait_ge(vec.sem, vec.at(g, "lo0", 10))
                            if s == 1:
                                te.wait_ge(vec.sem, vec.at(g, "lo1", 10))
                        elif s % 2 == 0:
                            te.wait_ge(act.sem, act.at(d, f"sq{p}", i - 1))
                        for kk in range(HALF):
                            kc = HALF * (s % 2) + kk
                            last = product(bank[2 * p][:, 0:T], s, kk, a_hi[:, kc, :], a_lo[:, kc, :],
                                           kc == 0, kc == FC - 1)
                        last.then_inc(unit_done, 1)
                quads(d, dn_quad)
                ada(k, 11).then_inc(pe.step(d, "ada"), 1)
                res(f"res{k}", pool.at(d + "t", "add0"), act.at(d, "sq1", 3))

            def evac_free(stage):
                return lambda s, i: (act.sem, act.at(stage, f"e{s}", i))

            def out1(stage, res_, ready):
                project(stage, T, a_hi, a_lo, lambda s, i: (act.sem, act.at(stage, f"sq{s}", i)), after=ready)
                res(res_, pool.at(stage, "add6"), act.at(stage, "sq3", 1))

            te.wait_ge(pool.sem, pool.at("setup", "ones"))
            te.wait_ge(vec.sem, vec.at("setup", "lam"))
            te.matmul(bank[7][:, 0:2], ones[:, :], lam_pair[:, :], start=True, stop=True).then_inc(pe.step("setup", "lams"), 1)
            te.wait_ge(act.sem, act.at("setup", "cond"))

            ffn(0)
            if stop == "dn0": return
            pre("prec")
            project("cin", T, x_hi, x_lo, evac_free("cin"), k_ready=lo_ready("prec"))
            out1("cout", "resc", (vec.sem, vec.at("conv", "lo")))
            if stop == "cout": return
            ffn(1)
            ffn(2)
            pre("prea")
            project("ain", T, x_hi, x_lo, evac_free("ain"), k_ready=lo_ready("prea"))

            with te.Fori(0, HEADS) as hd:
                te.wait_ge(act.sem, act.at("ain", "e3", 5))
                te.wait_ge(vec.sem, vec.at("att", "full", hd - 1))
                te.matmul(bank[0][:, 0:T], con("ropeswap"), arena[:, bass.ds(hd * T, T)], start=True, stop=True
                          ).then_inc(pe.step("att", "pq"), 1)
                te.matmul(bank[1][:, 0:T], con("ropeswap"), arena[:, bass.ds((8 + hd) * T, T)], start=True, stop=True
                          ).then_inc(pe.step("att", "pk"), 1)
                te.wait_ge(act.sem, act.at("att", "vs", hd))
                te.transpose(bank[2][:, 0:P], vs[:, 0:P], ident)
                te.transpose(bank[2][:, P:2 * P], vs[:, P:2 * P], ident)
                te.transpose(bank[2][0:META, 2 * P:3 * P], vs[:, 256:T], ident).then_inc(pe.step("att", "vt"), 1)
                te.wait_ge(vec.sem, vec.at("att", "ks", hd))
                for qb in range(3):
                    q0 = P * qb
                    n_q = P if qb < 2 else META
                    n_k = P * (qb + 1) if qb < 2 else T
                    for c in range(2):
                        dst = (bank[4][:, c * P:(c + 1) * P], bank[5][:, c * 256:(c + 1) * 256],
                               bank[6 + c][:, 0:T])[qb]
                        te.matmul(dst[0:n_q, :], q_half[:, c, q0:q0 + n_q], ks[:, 0:n_k],
                                  start=True, stop=False)
                        last = te.matmul(dst[0:n_q, q0:q0 + n_q], ident[0:n_q, 0:n_q], con("causal")[0:n_q, 0:n_q],
                                         start=False, stop=True)
                        if qb == 2:
                            last.then_inc(pe.step("att", f"s{2 + c}"), 1)
                    if qb < 2:
                        last.then_inc(pe.step("att", f"s{qb}"), 1)
                te.wait_ge(vec.sem, vec.at("att", "a0", hd))
                te.transpose(bank[3][:, 0:P], f[:, 0, 0:P], ident).then_inc(pe.step("att", "t0"), 1)
                te.wait_ge(vec.sem, vec.at("att", "a1", hd))
                te.transpose(bank[4][:, 0:P], f[:, 2, 0:P], ident)
                te.transpose(bank[4][:, P:2 * P], f[:, 2, P:2 * P], ident).then_inc(pe.step("att", "t1"), 1)
                te.wait_ge(vec.sem, vec.at("att", "a2", hd))
                te.matmul(bank[0][:, 0:16], f[0:META, 4, 0:P], ident[0:META, 0:META], start=True, stop=True)
                te.matmul(bank[0][:, 16:32], f[0:META, 4, P:2 * P], ident[0:META, 0:META], start=True, stop=True)
                te.matmul(bank[0][0:META, 32:48], f[0:META, 4, 256:T], ident[0:META, 0:META], start=True, stop=True
                          ).then_inc(pe.step("att", "t2"), 1)
                at_ = f[:, 6:8, :]
                te.wait_ge(act.sem, act.at("att", "at3", hd))
                te.matmul(bank[1][:, 0:T], vn[:, 0, :], at_[:, 0, :], start=True, stop=False)
                te.matmul(bank[1][:, P:T], vn[:, 1, :], at_[:, 1, P:T], start=False, stop=False)
                te.matmul(bank[1][:, 256:T], vn[0:META, 2, :], at2[:, :], start=False, stop=True
                          ).then_inc(pe.step("att", "o"), 1)
                te.wait_ge(act.sem, act.at("att", "osq", hd))
                te.matmul(bank[2][:, 0:T], ones[:, :], sq[:, 0, :], start=True, stop=True).then_inc(pe.step("att", "oss"), 1)

            out1("aout", "resa", (vec.sem, vec.at("att", "lo", HEADS - 1)))
            if stop == "aout": return
            ffn(3)
            if stop == "dn3": return
            pre("pree")
            project("ein", SEQ, x_hi, x_lo, evac_free("ein"), k_ready=lo_ready("pree"))

            ar = arena[:, 0:32 * SEQ]
            te.wait_ge(act.sem, act.at("ein", "e3", 5))
            for j in range(2):
                for a in range(4):
                    g = 4 * j + a
                    last = te.transpose(bank[6 + j][:, a * P:(a + 1) * P], ar[:, 8 * SEQ + g * P:8 * SEQ + (g + 1) * P], ident)
                last.then_inc(pe.step("hg", f"vt{j}"), 1)
            key, qp, q_ = ar[:, 24 * SEQ:28 * SEQ], ar[:, 28 * SEQ:32 * SEQ], ar[:, 0:4 * SEQ]
            te.wait_ge(vec.sem, vec.at("hg", "key"))
            for g in range(8):
                last = te.matmul(bank[g // 4][:, (g % 4) * P:(g % 4 + 1) * P], key[:, g * P:(g + 1) * P],
                                 q_[:, g * P:(g + 1) * P], start=True, stop=True)
            last.then_inc(pe.step("hg", "dg"), 1)
            for i in range(LEVELS):
                b = 1 << i
                if i == 0:
                    te.wait_ge(vec.sem, vec.at("hg", "q0"))
                else:
                    te.wait_ge(vec.sem, vec.at("hg", f"kp{i - 1}"))
                qv = qp.rearrange("p (g n r b) -> p g n r b", g=8, r=2, b=b)
                for g in range(8):
                    last = te.matmul(bank[2 + i % 2][:, g * 64:(g + 1) * 64], key[:, g * P:(g + 1) * P],
                                     qv[:, g, :, 1, :], start=True, stop=True)
                last.then_inc(pe.step("hg", f"lv{i}"), 1)
            te.wait_ge(vec.sem, vec.at("hg", f"kp{LEVELS - 1}"))
            te.wait_ge(act.sem, act.at("hg", "vn1"))
            for a in range(4):
                last = te.matmul(bank[6][:, a * P:(a + 1) * P], key[:, 2 * a * P:(2 * a + 1) * P],
                                 qp[:, (2 * a + 1) * P:(2 * a + 2) * P], start=True, stop=True)
            last.then_inc(pe.step("hg", f"lv{LEVELS}"), 1)
            i_tok = ar[:, 8 * SEQ:12 * SEQ]
            st = ar[:, 0:4 * SEQ]
            te.wait_ge(act.sem, act.at("hg", "s2"))
            te.wait_ge(vec.sem, vec.at("hg", f"cp{LEVELS - 1}"))
            for a in range(4):
                v0, v1 = i_tok[:, 2 * a * P:(2 * a + 1) * P], i_tok[:, (2 * a + 1) * P:(2 * a + 2) * P]
                te.matmul(bank[a][:, 0:P], v0, st[:, 2 * a * P:(2 * a + 1) * P], start=True, stop=True)
                te.matmul(bank[a][:, P:2 * P], v0, xt[:, a // 2, (a % 2) * P:(a % 2 + 1) * P], start=True, stop=False)
                te.matmul(bank[a][:, P:2 * P], v1, st[:, (2 * a + 1) * P:(2 * a + 2) * P], start=False, stop=True
                          ).then_inc(pe.step("hg", f"pv{a}"), 1)
            for a in range(4):
                te.wait_ge(act.sem, act.at("hg", f"sq{a}"))
                if a >= 2:
                    te.wait_ge(act.sem, act.at("hg", f"ln{a - 2}"))
                te.matmul(bank[4 + a % 2][:, 0:SEQ], ones[:, :], silu_t[:, a % 2, 0:SEQ], start=True, stop=True
                          ).then_inc(pe.step("hg", f"ss{a}"), 1)
            for g in range(4):
                te.wait_ge(pool.sem, pool.at("hg", f"p{g}"))
                if g >= 2:
                    te.wait_ge(vec.sem, vec.at("hg", f"on{g + 2}"))
                te.matmul(bank[6 + g % 2][:, 0:SEQ], poolw[:, g, :], (pool_a, pool_b)[g % 2][:, g, :], start=True, stop=True
                          ).then_inc(pe.step("hg", f"pl{g}"), 1)

            project("eout", SEQ, a_hi, a_lo, lambda s, i: (vec.sem, vec.at("eout", f"h{s}", i)),
                    after=(vec.sem, vec.at("hg", "lo7")))
            if stop == "eout": return
            pre("preo")
            project("oin", SEQ, x_hi, x_lo, evac_free("oin"), k_ready=lo_ready("preo"))

            te.wait_ge(vec.sem, vec.at("fl", "wlo"))
            te.wait_ge(act.sem, act.at("oin", "e3", 7))
            for j in range(2):
                for k in range(DC):
                    ts = slice(j * P, (j + 1) * P)
                    te.matmul(bank[j][:, 0:16], x_hi[:, k, ts], flw_hi[:, k, :], start=(k == 0), stop=False)
                    te.matmul(bank[j][:, 0:16], x_hi[:, k, ts], flw_lo[:, k, :], start=False, stop=False)
                    last = te.matmul(bank[j][:, 0:16], x_lo[:, k, ts], flw_hi[:, k, :], start=False, stop=(k == DC - 1))
            last.then_inc(pe.step("fl", "fl"), 1)
            te.wait_ge(act.sem, act.at("fl", "cp1"))
            te.transpose(bank[2][0:16, 0:P], small[:, 0:16], ident)
            te.transpose(bank[2][0:16, P:2 * P], small[:, 16:32], ident).then_inc(pe.step("fl", "tr"), 1)

            with te.Fori(0, 8) as j:
                te.wait_ge(act.sem, act.at("fox", "sqq", j))
                te.matmul(bank[0][:, 0:SEQ], con("ones64"), sq[:, 0, 0:SEQ], start=True, stop=True).then_inc(pe.step("fox", "nq"), 1)
                te.wait_ge(act.sem, act.at("fox", "sqk", j))
                te.matmul(bank[0][:, SEQ:512], con("ones64"), sq[:, 1, 0:SEQ], start=True, stop=True).then_inc(pe.step("fox", "nk"), 1)
                te.wait_ge(act.sem, act.at("fox", "vs", j))
                te.wait_ge(vec.sem, vec.at("fl", "z"))
                te.transpose(bank[2][:, 0:P], vs[:, 0:P], ident)
                te.transpose(bank[2][:, P:2 * P], vs[:, P:2 * P], ident).then_inc(pe.step("fox", "vt"), 1)
                te.wait_ge(vec.sem, vec.at("fox", "d1", j))
                te.wait_ge(act.sem, act.at("fox", "e11", j - 1))
                for qb in range(2):
                    n_k = P * (qb + 1)
                    for e in range(2):
                        dst = bank[4 + qb][:, e * n_k:(e + 1) * n_k]
                        te.matmul(dst, ones[0:16, :], lnb[0:16, e, 0:n_k], start=True, stop=False)
                        te.matmul(dst, q_half[:, e, qb * P:(qb + 1) * P], ks[:, 0:n_k],
                                  start=False, stop=False)
                        last = te.matmul(dst[:, qb * P:n_k], ident, con("causal"), start=False, stop=True)
                    last.then_inc(pe.step("fox", f"s{qb}"), 1)
                te.wait_ge(act.sem, act.at("fox", "pt1", j - 1))
                te.wait_ge(vec.sem, vec.at("fox", "p01", j))
                te.transpose(bank[6][:, 0:P], pool_a[:, 0, 0:P], ident)
                te.transpose(bank[6][:, P:2 * P], pool_a[:, 1, 0:P], ident).then_inc(pe.step("fox", "t0"), 1)
                te.wait_ge(vec.sem, vec.at("fox", "p11", j))
                for e in range(2):
                    for kb in range(2):
                        last = te.transpose(bank[7][:, (2 * e + kb) * P:(2 * e + kb + 1) * P], pool_a[:, 2 + e, kb * P:(kb + 1) * P], ident)
                last.then_inc(pe.step("fox", "t1"), 1)
                te.wait_ge(act.sem, act.at("fox", "pt1", j))
                te.wait_ge(vec.sem, vec.at("fox", "full", j - 1))
                for e in range(2):
                    ps = slice(64 * e, 64 * e + 64)
                    te.matmul(bank[3][ps, 0:P], vn[:, 0, ps], xt[:, 0, e * P:(e + 1) * P], start=True, stop=True)
                    te.matmul(bank[3][ps, P:2 * P], vn[:, 0, ps], silu_t[:, e, 0:P], start=True, stop=False)
                    last = te.matmul(bank[3][ps, P:2 * P], vn[:, 1, ps], silu_t[:, e, P:2 * P], start=False, stop=True)
                last.then_inc(pe.step("fox", "o"), 1)

            project("oout", SEQ, a_hi, a_lo, lambda s, i: (vec.sem, vec.at("oout", f"h{s}", i)),
                    after=(vec.sem, vec.at("fox", "lo", 7)))


def unit_tiles(w):
    k, n = w.shape
    return w.reshape(k // P, P, n // P, P).transpose(2, 1, 0, 3).reshape(n // P, P, (k // P) * P)


def interleave(*groups):
    return np.stack(groups, axis=1).reshape(-1, *groups[0].shape[1:])


def gate_up(w):
    u = unit_tiles(w)
    return interleave(u[:FC], u[FC:])


def down(w):
    u = w.reshape(2, HALF, P, DC, P).transpose(3, 0, 2, 1, 4)
    return u.reshape(2 * DC, P, W11)


def columns(v):
    return v.reshape(-1, P).T


def padded(v):
    out = np.zeros((P, v.shape[1]), v.dtype)
    out[:v.shape[0]] = v
    return out


def constants():
    c = np.zeros((P, N_CONSTS), np.float32)

    def put(name, value):
        a, n = CONSTS[name]
        c[:value.shape[0], a:a + n] = value
    put("ident", np.eye(P, dtype=np.float32))
    swap = np.zeros((P, P), np.float32)
    cos, sin = np.ones((P, T), np.float32), np.zeros((P, T), np.float32)
    inv = np.float32(500000.0) ** (-np.arange(0, 16, 2, dtype=np.float32) / np.float32(16))
    ang = np.arange(T, dtype=np.float32)[None, :] * inv[:, None].astype(np.float32)
    for s in range(2):
        for i in range(8):
            a, b = 64 * s + i, 64 * s + 8 + i
            swap[b, a], swap[a, b] = -1.0, 1.0
            cos[a], cos[b] = np.cos(ang[i]), np.cos(ang[i])
            sin[a], sin[b] = np.sin(ang[i]), np.sin(ang[i])
    put("ropeswap", swap)
    put("cos", cos)
    put("sin", sin)
    put("causal", np.where(np.arange(P)[None, :] <= np.arange(P)[:, None], 0.0, NEG).astype(np.float32))
    put("ones64", (np.arange(P)[:, None] // 64 == np.arange(P)[None, :] // 64).astype(np.float32))
    put("pick", np.eye(16, dtype=np.float32))
    w = 2 << np.arange(4)
    put("invcount", np.tile((1.0 / np.minimum(np.arange(16)[None, :] + 1, w[:, None])).reshape(1, 64), (P, 1)).astype(np.float32))
    m = np.zeros((P, LEVELS, 64), np.int32)
    for i in range(LEVELS):
        b = 1 << i
        t = np.array([2 * b * n + b + r for n in range(64 // b) for r in range(b)])
        s = np.arange(P)
        m[:, i] = (s[:, None] // (2 * b) == t[None, :] // (2 * b)) & (s[:, None] % (2 * b) < b)
    return c, m


def layout(i):
    w8 = [gate_up(i["ffn1_w_gu"][0])]
    u = unit_tiles(i["conv_w_in"][0])
    w8 += [u[8:24], u[0:8], unit_tiles(i["conv_w_out"][0]), gate_up(i["ffn2_w_gu"][0]), gate_up(i["ffn1_w_gu"][1]),
           unit_tiles(i["attn_w_qkv"][0]), unit_tiles(i["attn_w_o"][0]), gate_up(i["ffn2_w_gu"][1]),
           unit_tiles(i["even_w_in_2"][0]), unit_tiles(i["even_w_out_2"][0]),
           unit_tiles(i["odd_w_in_2"][0][:, :4 * D]), unit_tiles(i["odd_w_out_2"][0])]
    w11 = [down(i["ffn1_w_down"][0]), down(i["ffn2_w_down"][0]), down(i["ffn1_w_down"][1]), down(i["ffn2_w_down"][1])]
    ada = np.concatenate([unit_tiles(i["ada_w_2"][l]) for l in range(2)]).reshape(48, P, DC, P)
    p = {
        "ln_ffn1": columns(i["ln_ffn1"].reshape(-1)), "ln_mix": columns(i["ln_mix"].reshape(-1)),
        "ln_ffn2": columns(i["ln_ffn2"].reshape(-1)), "conv_w": columns(i["conv_w"].reshape(-1)),
        "subln_g": columns(i["attn_subln_g"].reshape(-1)), "lam": padded(i["attn_lambda"][0].T),
        "c": columns(i["c_2"].reshape(-1)), "norm_g": columns(i["norm_g_2"].reshape(-1)),
        "ada_b": columns(i["ada_b_2"].reshape(-1)), "hgrn_lb": columns(i["hgrn_lb_2"].reshape(-1)),
        "onorm_g": columns(i["hgrn_onorm_g_2"].reshape(-1)), "pool_scale": columns(i["pool_scale_2"].reshape(-1)),
        "qnorm_g": np.tile(i["fox_qnorm_g_2"][0], 2)[:, None], "knorm_g": np.tile(i["fox_knorm_g_2"][0], 2)[:, None],
        "b_f": padded(i["fox_b_f_2"].T),
    }
    c, m = constants()
    x = np.concatenate([i["meta_tokens"], i["x"][0]]).T.reshape(DC, P, T).transpose(1, 0, 2)
    return {
        "w8": np.concatenate(w8), "w11": np.concatenate(w11), "ada_w": ada,
        "params": np.concatenate([p[n] for n in PARAMS], axis=1), "consts": c, "level_masks": m,
        "pool_w": i["pool_w_2"][0].transpose(1, 0, 2),
        "fl_w": i["odd_w_in_2"][0][:, 4 * D:].reshape(DC, P, 16).transpose(1, 0, 2),
        "x_in": x,
    }


def kernel(**inputs):
    import concourse.bacc as bacc
    from concourse.bass_utils import run_bass_kernel_spmd

    nc = bacc.Bacc("TRN2", target_bir_lowering=False, num_devices=1)
    arrays = {n: np.ascontiguousarray(a) for n, a in layout({n: np.asarray(a) for n, a in inputs.items()}).items()}
    args = [nc.dram_tensor(n, a.shape, mybir.dt.from_np(a.dtype), kind="ExternalInput").ap() for n, a in arrays.items()]
    out = nc.dram_tensor("out", (P, DC, SEQ), F32, kind="ExternalOutput").ap()
    build(nc, *args, out)
    r = run_bass_kernel_spmd(nc, [arrays], core_ids=[0])
    got = r.results[0]["out"]
    return np.ascontiguousarray(got.transpose(1, 0, 2).reshape(1, D, SEQ).transpose(0, 2, 1))
```

```python
import numpy as np
import concourse.bass as bass
from concourse import mybir
from contextlib import ExitStack

F32 = mybir.dt.float32
F32R = mybir.dt.float32r
I32 = mybir.dt.int32
ALU = mybir.AluOpType
ACT = mybir.ActivationFunctionType
AX = mybir.AxisListType

P = 128
D = 1024
DC = D // P
META = 16
SEQ = 256
T = META + SEQ
FF = 2816
FC = FF // P
HALF = FC // 2
W8, W11 = DC * P, HALF * P
SLOTS = 4
HEADS = 8
LEVELS = 7
LAMBDA_INIT = 0.8 - 0.6 * float(np.exp(-0.3))
NEG = -1e30

STAGES = [("gu0", 11), ("dn0", 4), ("cin", 6), ("cout", 2), ("gu1", 11), ("dn1", 4),
          ("gu2", 11), ("dn2", 4), ("ain", 6), ("aout", 2), ("gu3", 11), ("dn3", 4),
          ("ein", 6), ("eout", 2), ("oin", 8), ("oout", 2)]
QUADS = dict(STAGES)
FIRST_QUAD = {}
_q = 0
for _name, _n in STAGES:
    FIRST_QUAD[_name] = _q
    _q += _n
ALL_QUADS = _q


def wide(stage):
    return stage.startswith("dn")


def unit_base(stage):
    at = 0
    for name, n in STAGES:
        if name == stage:
            return at
        if wide(name) == wide(stage):
            at += SLOTS * n
    return at


def stage_after(stage):
    names = [n for n, _ in STAGES]
    i = names.index(stage) + 1
    return names[i] if i < len(names) else None


PARAMS, _n = {}, 0
for _name, _count in [("ln_ffn1", 32), ("ln_mix", 32), ("ln_ffn2", 32), ("conv_w", 24), ("subln_g", 1),
                      ("lam", 4), ("c", 8), ("norm_g", 16), ("ada_b", 48), ("hgrn_lb", 12), ("onorm_g", 4),
                      ("pool_scale", 4), ("qnorm_g", 1), ("knorm_g", 1), ("b_f", 1)]:
    PARAMS[_name] = (_n, _count)
    _n += _count
N_PARAMS = _n

CONSTS, _n = {}, 0
for _name, _count in [("ident", P), ("ropeswap", P), ("causal", P), ("ones64", P), ("cos", T), ("sin", T),
                      ("pick", 16), ("invcount", 4 * 16)]:
    CONSTS[_name] = (_n, _count)
    _n += _count
N_CONSTS = _n


class Steps:

    def __init__(self, sem):
        self.sem, self.total, self.phases, self.now = sem, 0, {}, {}

    def phase(self, name, steps, times=1):
        self.phases[name] = (self.total, steps, times)
        self.total += len(steps) * times

    def at(self, phase, step, i=0):
        base, steps, _ = self.phases[phase]
        return base + len(steps) * i + steps.index(step) + 1

    def step(self, phase, step):
        _, steps, _ = self.phases[phase]
        k = self.now.get(phase, 0)
        assert steps[k % len(steps)] == step, (phase, step, steps[k % len(steps)])
        self.now[phase] = k + 1
        return self.sem


def build(nc, w8, w11, ada_w, params_in, consts_in, masks_in, pool_w, fl_w, x_in, out):
    ctx = ExitStack()
    with ctx:
        def sb(name, shape, dt=F32):
            return ctx.enter_context(nc.sbuf_tensor(name, shape, dt))

        def sem(name):
            return ctx.enter_context(nc.semaphore(name))

        raw = sb("raw", [P, SLOTS, W11])
        w_hi = sb("w_hi", [P, SLOTS, W11], F32R)
        w_lo = sb("w_lo", [P, SLOTS, W11], F32R)
        ada_raw = sb("ada_raw", [P, DC, P])
        h = sb("h", [P, DC, T])
        x_hi = sb("x_hi", [P, DC, T], F32R)
        x_lo = sb("x_lo", [P, DC, T], F32R)
        a_hi = sb("a_hi", [P, FC, T], F32R)
        a_lo = sb("a_lo", [P, FC, T], F32R)
        arena = sb("arena", [P, 32 * T])
        f = arena[:, 24 * T:32 * T].rearrange("p (c t) -> p c t", c=DC)
        xt = sb("xt", [P, 2, T])
        silu_t = sb("silu_t", [P, 2, T])
        sq = sb("sq", [P, 2, T])
        sq_sum = sb("sq_sum", [P, T])
        ln_t = sb("ln_t", [P, 512])
        r_t = sb("r_t", [P, 512])
        prm = sb("prm", [P, N_PARAMS])
        cst = sb("cst", [P, N_CONSTS])
        lvl_mask = sb("lvl_mask", [P, LEVELS, 64], I32)
        poolw = sb("poolw", [P, 4, P])
        flw = sb("flw", [P, DC, 16])
        flw_hi = sb("flw_hi", [P, DC, 16], F32R)
        flw_lo = sb("flw_lo", [P, DC, 16], F32R)
        ones = sb("ones", [P, P])
        eps6 = sb("eps6", [P, 1])
        eps5 = sb("eps5", [P, 1])
        one = sb("one", [P, 1])
        half_g = sb("half_g", [P, 4, DC])
        sub_g = sb("sub_g", [P, 1])
        gq = sb("gq", [P, 1])
        lam_pair = sb("lam_pair", [P, 2])
        lam_exp = sb("lam_exp", [P, 2])
        neg_lam = sb("neg_lam", [P, 1])
        cond = sb("cond", [P, DC])
        mod = sb("mod", [P, 2, 3, DC])
        gs = sb("gs", [P, 2, DC])
        lb = sb("lb", [P, 2, 4])
        lb3 = sb("lb3", [P, 3, 4])
        lbm = sb("lbm", [P, 4])
        work = sb("work", [P, 4, T])
        qs, ks, vs = (work[:, i, :] for i in range(3))
        q_half = sb("q_half", [P, 2, T])
        vn = sb("vn", [P, 3, P])
        small = sb("small", [P, 32])
        ada_sum = vn[:, 0, :]
        at2 = sb("at2", [META, META])
        pool_a = ada_raw[:, :, :].rearrange("p a b -> p (a b)").rearrange("p (g t) -> p g t", g=4)
        pool_b = work[:, :, 0:SEQ]
        lnb = poolw[0:16, :, :].rearrange("p a b -> p (a b)").rearrange("p (e k) -> p e k", e=2)

        bank = [ctx.enter_context(nc.psum_tensor(f"bank{i}", [P, 512], F32)) for i in range(8)]
        STAT, ADA = bank[4], bank[5]

        raw_in = [sem(f"raw_in{s}") for s in range(SLOTS)]
        w_hi_ready, w_lo_ready, unit_done = sem("w_hi_ready"), sem("w_lo_ready"), sem("unit_done")
        ada_in, setup_in, out_done = sem("ada_in"), sem("setup_in"), sem("out_done")
        act_b, vec_b, pe_b = (Steps(sem(n)) for n in ("scalar_softmax_steps", "vector_softmax_steps", "tensor_softmax_steps"))
        act, vec, pe, pool = (Steps(sem(n)) for n in ("scalar_steps", "vector_steps", "tensor_steps", "gpsimd_steps"))

        def par(name, i=0, n=1):
            a = PARAMS[name][0] + i
            return prm[:, a:a + n]

        def con(name):
            a, n = CONSTS[name]
            return cst[:, a:a + n]

        ident = con("ident")
        CH = [str(c) for c in range(DC)]

        def lagged(first, second, n=DC):
            out_ = []
            for c in range(n + 1):
                if c < n:
                    out_.append((first, c))
                if c:
                    out_.append((second, c - 1))
            return out_

        def names(pairs):
            return [a + str(c) for a, c in pairs]

        pool.phase("setup", ["ones", "eps6", "eps5", "one", "q_half"])
        vec.phase("setup", ["lam", "half0", "half1", "half2", "half3", "subg", "gq", "lbm", "lb0", "lb1", "lb2",
                            "lbs", "lbt", "lbr", "lbq", "lbn", "lamd", "laml"])
        act.phase("setup", ["cond", "lame", "lbe"])
        pe.phase("setup", ["lams"])

        def declare_pre(n):
            act.phase(n, names([("sq", c) for c in range(DC)]) + ["ln", "r"] + names([("hi", c) for c in range(DC)]))
            pe.phase(n, names([("ss", c) for c in range(DC)]))
            vec.phase(n, (["gs"] if n in ("pree", "preo") else []) + names(lagged("t", "lo")))

        def declare_res(n):
            pe.phase(n, ["ss"])
            act.phase(n, ["ln", "r"])
            vec.phase(n, names(lagged("t", "h")))

        def declare_ffn(k):
            declare_pre(f"pre{k}")
            g, d = f"gu{k}", f"dn{k}"
            act.phase(g, ["silu0", "silu1"], 11)
            vec.phase(g, ["am", "ar", "hi0", "full0", "lo0", "hi1", "full1", "lo1"], 11)
            pe.phase(g, ["ada"], 11)
            act.phase(d, ["f0", "sq0", "f1", "sq1"], 4)
            pool.phase(d, ["zero"])
            pool.phase(d + "s", ["add0", "add1"], 3)
            pool.phase(d + "t", ["add0"])
            pe.phase(d, ["ada"])
            vec.phase(d, ["am", "ar", "mod"])
            declare_res(f"res{k}")

        def declare_out1(n, res):
            act.phase(n, ["f0", "sq0", "f1", "sq1", "f2", "sq2", "f3", "sq3"], 2)
            pool.phase(n, ["zero"] + [f"add{o}" for o in range(7)])
            declare_res(res)

        declare_ffn(0)
        declare_pre("prec")
        act.phase("cin", ["e0", "e1", "e2", "e3"], 6)
        vec.phase("conv", ["u"] + ["w2" + c for c in CH] + ["w1" + c for c in CH] + ["w0" + c for c in CH]
                  + ["hi", "full", "lo"])
        declare_out1("cout", "resc")
        declare_ffn(1)
        declare_ffn(2)
        declare_pre("prea")
        act.phase("ain", ["e0", "e1", "e2", "e3"], 6)
        pe.phase("att", ["pq", "pk", "vt"], HEADS)
        vec.phase("att", ["qc", "kc", "qx", "kx", "qs0", "qs1", "ks"], HEADS)
        act.phase("att", ["vs", "vn", "vn2"], HEADS)
        pe_b.phase("att", ["s0", "s1", "s2", "s3", "t0", "t1", "t2", "o", "oss"], HEADS)
        vec_b.phase("att", ["m0", "n0", "m1", "n1", "m2", "m3", "n2", "r0", "l0", "b0", "a0", "r1", "l1", "b1", "a1",
                            "r2", "l2", "b2", "a2", "hi", "full", "lo"], HEADS)
        act_b.phase("att", ["e00", "e01", "e10", "e11", "e20", "e21", "at0", "at1", "at2", "at3", "osq", "ln", "r"], HEADS)
        declare_out1("aout", "resa")
        declare_ffn(3)
        declare_pre("pree")
        act.phase("ein", ["e0", "e1", "e2", "e3"], 6)
        act.phase("hg", ["sig", "sga", "sgb", "vn0", "vn1", "s2"] + [f"{a}{i}" for i in range(4) for a in ("sq", "ln", "r")])
        lv = []
        for i in range(LEVELS):
            lv += [f"cp{i}", f"qp{i}", f"kp{i}", f"tp{i}"]
        vec.phase("hg", ["fg0", "fg1", "fg2", "fg3", "key", "fm", "q0", "dg0", "dg1"] + lv
                  + [f"{a}{i}" for i in range(4) for a in ("on", "hi", "full", "lo")]
                  + [f"{a}{i}" for i in range(4, 8) for a in ("on", "hi", "full", "lo")])
        pe.phase("hg", ["vt0", "vt1", "dg"] + [f"lv{i}" for i in range(LEVELS + 1)] + ["pv0", "pv1", "pv2", "pv3"]
                 + [f"ss{i}" for i in range(4)] + [f"pl{i}" for i in range(4)])
        pl = []
        for lvl in range(4):
            pl += [f"c{lvl}", f"s{lvl}"]
        pool.phase("hg", pl + [f"i{g}" for g in range(4)] + [f"j{g}" for g in range(4)] + [f"p{g}" for g in range(4)])
        vec.phase("eout", ["h0", "h1", "h2", "h3"], 2)
        declare_pre("preo")
        act.phase("oin", ["e0", "e1", "e2", "e3"], 8)
        act.phase("fl", ["whi", "sg", "cp0", "cp1", "exp", "ln"])
        vec.phase("fl", ["wlo", "z", "nz", "az", "logf", "cum", "ncum"])
        pe.phase("fl", ["fl", "tr"])
        act.phase("fox", ["sqq", "sqk", "vs", "ln", "r", "vn"], 8)
        vec.phase("fox", ["qn0", "qn1", "kn", "d0", "d1"], 8)
        pe.phase("fox", ["nq", "nk", "vt"], 8)
        act_b.phase("fox", ["e00", "e01", "e10", "e11", "pt0", "pt1"], 8)
        vec_b.phase("fox", ["m0", "n0", "m1", "n1", "r0", "p00", "p01", "r1", "p10", "p11", "hi", "full", "lo"], 8)
        pe_b.phase("fox", ["s0", "s1", "t0", "t1", "o"], 8)
        vec.phase("oout", ["h0", "h1", "h2", "h3"], 2)

        H_READY = {"pre0": None, "prec": ("res0", "h"), "pre1": ("resc", "h"), "pre2": ("res1", "h"),
                   "prea": ("res2", "h"), "pre3": ("resa", "h"), "pree": ("res3", "h"), "preo": ("eout", None)}
        GAIN = {"pre0": ("ln_ffn1", 0), "res0": ("half", 0), "prec": ("ln_mix", 0), "resc": ("ln_mix", 8),
                "pre1": ("ln_ffn2", 0), "res1": ("half", 1), "pre2": ("ln_ffn1", 16), "res2": ("half", 2),
                "prea": ("ln_mix", 16), "resa": ("ln_mix", 24), "pre3": ("ln_ffn2", 16), "res3": ("half", 3)}

        def gain(phase, c):
            name, first = GAIN[phase]
            return half_g[:, first, c:c + 1] if name == "half" else par(name, first + c)

        def tok(phase):
            return slice(META, T) if phase in ("pree", "preo") else slice(0, T)

        IN_PRE = {"gu0": "pre0", "cin": "prec", "gu1": "pre1", "gu2": "pre2", "ain": "prea", "gu3": "pre3",
                  "ein": "pree", "oin": "preo"}

        def one_behind(eng, n, body):
            body(0, True, False)
            with eng.Fori(1, n - 1) as j:
                body(j, False, False)
            body(n - 1, False, True)

        block = ctx.enter_context(nc.Block())

        @block.sync
        def _(sp):
            sp.dma_start(prm[:, :], params_in).then_inc(setup_in, 16)
            sp.dma_start(h[:, :, :], x_in).then_inc(setup_in, 16)
            sp.dma_start(cst[:, :], consts_in).then_inc(setup_in, 16)
            sp.dma_start(lvl_mask[:, :, :], masks_in).then_inc(setup_in, 16)
            sp.dma_start(poolw[:, :, :], pool_w).then_inc(setup_in, 16)
            sp.dma_start(flw[:, :, :], fl_w).then_inc(setup_in, 16)

            def load(stage, i):
                src, n = (w11, W11) if wide(stage) else (w8, W8)
                q = FIRST_QUAD[stage] + i
                for s in range(SLOTS):
                    if not (isinstance(i, int) and q == 0):
                        sp.wait_ge(w_lo_ready, SLOTS * q - SLOTS + s + 1)
                    sp.dma_start(raw[:, s, 0:n],
                                 src[bass.ds(unit_base(stage) + SLOTS * i + s, 1), :, :].rearrange("a p n -> (a p) n")
                                 ).then_inc(raw_in[s], 16)

            def load_ada(k, i):
                if isinstance(i, int) and i == 0:
                    if k:
                        sp.wait_ge(vec.sem, vec.at(f"dn{k - 1}", "ar"))
                else:
                    sp.wait_ge(vec.sem, vec.at(f"gu{k}", "ar", i - 1))
                sp.dma_start(ada_raw[:, :, :], ada_w[bass.ds(12 * k + i, 1), :, :, :].rearrange("a p k n -> (a p) k n")
                             ).then_inc(ada_in, 16)

            for stage, n in STAGES:
                k = int(stage[-1]) if stage[:2] in ("gu", "dn") else None
                load(stage, 0)
                if stage[:2] == "gu":
                    load_ada(k, 0)
                if stage[:2] == "dn":
                    load_ada(k, 11)
                with sp.Fori(1, n) as i:
                    load(stage, i)
                    if stage[:2] == "gu":
                        load_ada(k, i)
            sp.wait_ge(vec.sem, vec.total)
            sp.dma_start(out, h[:, :, META:T]).then_inc(out_done, 16)
            sp.wait_ge(out_done, 16)

        @block.scalar
        def _(sc):
            def split_hi(stage, i, s):
                n = W11 if wide(stage) else W8
                q = FIRST_QUAD[stage] + i
                sc.wait_ge(raw_in[s], 16 * q + 16)
                if not (isinstance(i, int) and q == 0):
                    sc.wait_ge(unit_done, SLOTS * q - SLOTS + s + 1)
                sc.activation(w_hi[:, s, 0:n], raw[:, s, 0:n], ACT.Copy).then_inc(w_hi_ready, 1)

            def split_next(stage, i, s):
                if isinstance(i, int) and i == QUADS[stage] - 1:
                    nxt = stage_after(stage)
                    if nxt:
                        split_hi(nxt, 0, s)
                else:
                    split_hi(stage, i + 1, s)

            def quads(stage, body):
                body(0)
                if QUADS[stage] > 2:
                    with sc.Fori(1, QUADS[stage] - 1) as i:
                        body(i)
                body(QUADS[stage] - 1)

            def rsqrt(phase, src, n, scale, eps, ready):
                if phase.startswith("res") or phase in ("pre0", "preo"):
                    sc.preload_act_table_set("natural_log_exp_and_others")
                sc.wait_ge(*ready)
                sc.activation(ln_t[:, 0:n], src, ACT.Ln, bias=eps[:, :], scale=scale).then_inc(act.step(phase, "ln"), 1)
                sc.wait_ge(act.sem, act.at(phase, "ln"))
                sc.activation(r_t[:, 0:n], ln_t[:, 0:n], ACT.Exp, scale=-0.5).then_inc(act.step(phase, "r"), 1)

            def pre(phase):
                ts = tok(phase)
                n = ts.stop - ts.start
                for c in range(DC):
                    src = H_READY[phase]
                    if src and src[0] == "eout":
                        sc.wait_ge(vec.sem, vec.at("eout", f"h{c % 4}", c // 4))
                    elif src:
                        sc.wait_ge(vec.sem, vec.at(src[0], f"h{c}"))
                    if c >= 2:
                        sc.wait_ge(pe.sem, pe.at(phase, f"ss{c - 2}"))
                    sc.activation(sq[:, c % 2, 0:n], h[:, c, ts], ACT.Square).then_inc(act.step(phase, f"sq{c}"), 1)
                rsqrt(phase, STAT[:, 0:n], n, 1.0 / D, eps6, (pe.sem, pe.at(phase, "ss7")))
                for c in range(DC):
                    sc.wait_ge(vec.sem, vec.at(phase, f"t{c}"))
                    if n == T:
                        sc.activation(x_hi[:, c, 0:n], xt[:, c % 2, 0:n], ACT.Copy).then_inc(act.step(phase, f"hi{c}"), 1)
                    else:
                        l = 0 if phase == "pree" else 1
                        sc.activation(x_hi[:, c, 0:n], xt[:, c % 2, 0:n], ACT.Identity, bias=mod[:, l, 0, c:c + 1]
                                      ).then_inc(act.step(phase, f"hi{c}"), 1)

            def ffn(k):
                g, d = f"gu{k}", f"dn{k}"
                pre(f"pre{k}")
                sc.preload_act_table(ACT.Silu)

                def gu_quad(i):
                    q = FIRST_QUAD[g] + i
                    for p in range(2):
                        sc.wait_ge(unit_done, SLOTS * q + 2 * p + 1)
                        sc.wait_ge(vec.sem, vec.at(g, f"full{p}", i - 1))
                        sc.activation(silu_t[:, p, :], bank[2 * p][:, 0:T], ACT.Silu).then_inc(act.step(g, f"silu{p}"), 1)
                        split_next(g, i, 2 * p)
                        split_next(g, i, 2 * p + 1)

                quads(g, gu_quad)

                def dn_quad(i):
                    q = FIRST_QUAD[d] + i
                    for p in range(2):
                        o = 2 * i + p
                        split_next(d, i, 2 * p)
                        sc.wait_ge(unit_done, SLOTS * q + 2 * p + 2)
                        sc.activation(f[:, bass.ds(o, 1), :].rearrange("p a t -> p (a t)"), bank[2 * p][:, 0:T],
                                      ACT.Copy).then_inc(act.step(d, f"f{p}"), 1)
                        if not isinstance(i, int) or i > 0:
                            sc.wait_ge(pool.sem, pool.at(d + "s", f"add{p}", i - 1))
                        sc.activation(sq[:, p, :], bank[2 * p][:, 0:T], ACT.Square).then_inc(act.step(d, f"sq{p}"), 1)
                        split_next(d, i, 2 * p + 1)

                quads(d, dn_quad)
                rsqrt(f"res{k}", STAT[:, 0:T], T, 1.0 / D, eps6, (pe.sem, pe.at(f"res{k}", "ss")))

            def evacuate(stage, n):
                def quad(i):
                    q = FIRST_QUAD[stage] + i
                    for s in range(SLOTS):
                        sc.wait_ge(unit_done, SLOTS * q + s + 1)
                        sc.activation(arena[:, bass.ds((SLOTS * i + s) * n, n)], bank[s][:, 0:n], ACT.Copy
                                      ).then_inc(act.step(stage, f"e{s}"), 1)
                        split_next(stage, i, s)
                quads(stage, quad)

            def out1(stage, res):
                for i in range(2):
                    q = FIRST_QUAD[stage] + i
                    for s in range(SLOTS):
                        o = SLOTS * i + s
                        sc.wait_ge(unit_done, SLOTS * q + s + 1)
                        sc.activation(f[:, o, :], bank[s][:, 0:T], ACT.Copy).then_inc(act.step(stage, f"f{s}"), 1)
                        if o >= 2:
                            sc.wait_ge(pool.sem, pool.at(stage, f"add{o - 2}"))
                        sc.activation(sq[:, o % 2, :], bank[s][:, 0:T], ACT.Square).then_inc(act.step(stage, f"sq{s}"), 1)
                        split_next(stage, i, s)
                rsqrt(res, STAT[:, 0:T], T, 1.0 / D, eps6, (pe.sem, pe.at(res, "ss")))

            sc.wait_ge(setup_in, 96)
            sc.activation(cond[:, :], par("c", 0, DC), ACT.Silu).then_inc(act.step("setup", "cond"), 1)
            sc.wait_ge(pe.sem, pe.at("setup", "lams"))
            sc.activation(lam_exp[:, :], bank[7][:, 0:2], ACT.Exp).then_inc(act.step("setup", "lame"), 1)
            sc.wait_ge(vec.sem, vec.at("setup", "lb2"))
            sc.activation(lb3[:, :, :], lb3[:, :, :], ACT.Exp).then_inc(act.step("setup", "lbe"), 1)
            sc.wait_ge(pool.sem, pool.at("setup", "one"))
            for s in range(SLOTS):
                split_hi("gu0", 0, s)

            ffn(0)
            pre("prec")
            evacuate("cin", T)
            out1("cout", "resc")
            ffn(1)
            ffn(2)
            pre("prea")
            evacuate("ain", T)

            def att_v(hd):
                if not (isinstance(hd, int) and hd == 0):
                    sc.wait_ge(pe.sem, pe.at("att", "vt", hd - 1))
                sc.activation(vs[:, :], arena[:, bass.ds((16 + hd) * T, T)], ACT.Copy).then_inc(act.step("att", "vs"), 1)

            def att_vn(hd):
                sc.wait_ge(pe.sem, pe.at("att", "vt", hd))
                sc.activation(vn[:, 0:2, :].rearrange("p a v -> p (a v)"), bank[2][:, 0:256], ACT.Copy
                              ).then_inc(act.step("att", "vn"), 1)
                sc.activation(vn[0:META, 2, :], bank[2][0:META, 256:384], ACT.Copy).then_inc(act.step("att", "vn2"), 1)

            def att_head(hd, first, last):
                if not last:
                    att_v(hd + 1)
                for qb in range(3):
                    n_q = P if qb < 2 else META
                    n_k = P * (qb + 1) if qb < 2 else T
                    sc.wait_ge(vec_b.sem, vec_b.at("att", f"n{qb}", hd))
                    if not first:
                        sc.wait_ge(pe_b.sem, pe_b.at("att", f"t{qb}", hd - 1))
                    for c in range(2):
                        src = (bank[4][:, c * P:(c + 1) * P], bank[5][:, c * 256:(c + 1) * 256],
                               bank[6 + c][:, 0:T])[qb]
                        sc.activation(f[0:n_q, 2 * qb + c, 0:n_k], src[0:n_q, :], ACT.Exp, scale=0.125,
                                      bias=small[0:n_q, 8 + 2 * qb + c:9 + 2 * qb + c],
                                      accum_out=small[0:n_q, 16 + 2 * qb + c:17 + 2 * qb + c]
                                      ).then_inc(act_b.step("att", f"e{qb}{c}"), 1)
                at_ = f[:, 6:8, :]
                sc.wait_ge(pe_b.sem, pe_b.at("att", "t0", hd))
                sc.activation(at_[:, 0, 0:P], bank[3][:, 0:P], ACT.Copy).then_inc(act_b.step("att", "at0"), 1)
                sc.wait_ge(pe_b.sem, pe_b.at("att", "t1", hd))
                sc.activation(at_[:, 0:2, P:2 * P], bank[4][:, 0:2 * P].rearrange("p (k q) -> p k q", k=2), ACT.Copy
                              ).then_inc(act_b.step("att", "at1"), 1)
                sc.wait_ge(pe_b.sem, pe_b.at("att", "t2", hd))
                sc.activation(at_[:, 0:2, 256:T], bank[5][:, 0:32].rearrange("p (k q) -> p k q", k=2), ACT.Copy
                              ).then_inc(act_b.step("att", "at2"), 1)
                sc.activation(at2[:, :], bank[5][0:META, 32:48], ACT.Copy).then_inc(act_b.step("att", "at3"), 1)
                sc.wait_ge(pe_b.sem, pe_b.at("att", "o", hd))
                sc.activation(sq[:, 0, :], bank[6][:, 0:T], ACT.Square).then_inc(act_b.step("att", "osq"), 1)
                if not last:
                    att_vn(hd + 1)
                sc.wait_ge(pe_b.sem, pe_b.at("att", "oss", hd))
                sc.activation(ln_t[:, 0:T], bank[7][:, 0:T], ACT.Ln, bias=eps5[:, :], scale=1.0 / P
                              ).then_inc(act_b.step("att", "ln"), 1)
                sc.wait_ge(act_b.sem, act_b.at("att", "ln", hd))
                if not first:
                    sc.wait_ge(vec_b.sem, vec_b.at("att", "full", hd - 1))
                sc.activation(r_t[:, 0:T], ln_t[:, 0:T], ACT.Exp, scale=-0.5).then_inc(act_b.step("att", "r"), 1)

            sc.wait_ge(act.sem, act.at("ain", "e3", 5))
            att_v(0)
            att_vn(0)
            one_behind(sc, HEADS, att_head)
            out1("aout", "resa")
            ffn(3)
            pre("pree")
            evacuate("ein", SEQ)

            ar = arena[:, 0:32 * SEQ]
            sc.wait_ge(act.sem, act.at("ein", "e3", 5))
            sc.activation(ar[:, 4 * SEQ:8 * SEQ], ar[:, 4 * SEQ:8 * SEQ], ACT.Sigmoid).then_inc(act.step("hg", "sig"), 1)
            sc.activation(ar[:, 12 * SEQ:16 * SEQ], ar[:, 12 * SEQ:16 * SEQ], ACT.Silu).then_inc(act.step("hg", "sga"), 1)
            sc.activation(ar[:, 20 * SEQ:24 * SEQ], ar[:, 20 * SEQ:24 * SEQ], ACT.Silu).then_inc(act.step("hg", "sgb"), 1)
            i_tok = ar[:, 8 * SEQ:12 * SEQ]
            for j in range(2):
                sc.wait_ge(pe.sem, pe.at("hg", f"vt{j}"))
                if j == 0:
                    sc.wait_ge(pe.sem, pe.at("hg", "vt1"))
                sc.activation(i_tok[:, j * 512:(j + 1) * 512], bank[6 + j][:, :], ACT.Copy).then_inc(act.step("hg", f"vn{j}"), 1)
            sc.wait_ge(pe.sem, pe.at("hg", f"lv{LEVELS}"))
            sc.activation(xt[:, :, 0:256], bank[6][:, :].rearrange("p (a b) -> p a b", a=2), ACT.Copy
                          ).then_inc(act.step("hg", "s2"), 1)
            sc.preload_act_table_set("natural_log_exp_and_others")
            for i in range(4):
                sc.wait_ge(pe.sem, pe.at("hg", f"pv{i}"))
                if i >= 2:
                    sc.wait_ge(pe.sem, pe.at("hg", f"ss{i - 2}"))
                sc.activation(silu_t[:, i % 2, 0:SEQ], bank[i][:, 0:SEQ], ACT.Square).then_inc(act.step("hg", f"sq{i}"), 1)
                sc.wait_ge(pe.sem, pe.at("hg", f"ss{i}"))
                if i == 0:
                    sc.wait_ge(vec.sem, vec.at("hg", f"tp{LEVELS - 1}"))
                sc.activation(ln_t[:, 0:SEQ], bank[4 + i % 2][:, 0:SEQ], ACT.Ln, bias=eps6[:, :], scale=1.0 / P
                              ).then_inc(act.step("hg", f"ln{i}"), 1)
                sc.wait_ge(act.sem, act.at("hg", f"ln{i}"))
                if i >= 2:
                    sc.wait_ge(vec.sem, vec.at("hg", f"on{i - 2}"))
                sc.activation(r_t[:, (i % 2) * SEQ:(i % 2 + 1) * SEQ], ln_t[:, 0:SEQ], ACT.Exp, scale=-0.5
                              ).then_inc(act.step("hg", f"r{i}"), 1)

            def out2(stage):
                for i in range(2):
                    for s in range(SLOTS):
                        split_next(stage, i, s)

            out2("eout")
            pre("preo")
            evacuate("oin", SEQ)

            sc.activation(flw_hi[:, :, :], flw[:, :, :], ACT.Copy).then_inc(act.step("fl", "whi"), 1)
            sc.wait_ge(act.sem, act.at("oin", "e3", 7))
            sc.activation(ar[:, 24 * SEQ:32 * SEQ], ar[:, 24 * SEQ:32 * SEQ], ACT.Silu).then_inc(act.step("fl", "sg"), 1)
            sc.preload_act_table_set("natural_log_exp_and_others")
            sc.wait_ge(pe.sem, pe.at("fl", "fl"))
            for j in range(2):
                sc.activation(small[:, 16 * j:16 * j + 16], bank[j][:, 0:16], ACT.Copy).then_inc(act.step("fl", f"cp{j}"), 1)
            sc.wait_ge(vec.sem, vec.at("fl", "az"))
            sc.activation(pool_a[0:16, 3, :], pool_a[0:16, 2, :], ACT.Exp, scale=-1.0).then_inc(act.step("fl", "exp"), 1)
            sc.wait_ge(act.sem, act.at("fl", "exp"))
            sc.activation(pool_b[0:16, 0, :], pool_a[0:16, 3, :], ACT.Ln, bias=one[0:16, :]).then_inc(act.step("fl", "ln"), 1)

            def fox_squares(j):
                if not (isinstance(j, int) and j == 0):
                    sc.wait_ge(pe.sem, pe.at("fox", "nk", j - 1))
                sc.activation(sq[:, 0, 0:SEQ], ar[:, bass.ds(j * SEQ, SEQ)], ACT.Square).then_inc(act.step("fox", "sqq"), 1)
                sc.activation(sq[:, 1, 0:SEQ], ar[:, bass.ds((8 + j) * SEQ, SEQ)], ACT.Square).then_inc(act.step("fox", "sqk"), 1)
                sc.wait_ge(vec.sem, vec.at("fl", "ncum"))
                if not (isinstance(j, int) and j == 0):
                    sc.wait_ge(pe.sem, pe.at("fox", "vt", j - 1))
                sc.activation(vs[:, 0:SEQ], ar[:, bass.ds((16 + j) * SEQ, SEQ)], ACT.Copy).then_inc(act.step("fox", "vs"), 1)

            def fox_rms(j):
                sc.wait_ge(pe.sem, pe.at("fox", "nk", j))
                sc.activation(ln_t[:, :], bank[0][:, :], ACT.Ln, bias=eps6[:, :], scale=1.0 / 64).then_inc(act.step("fox", "ln"), 1)
                sc.wait_ge(act.sem, act.at("fox", "ln", j))
                if not (isinstance(j, int) and j == 0):
                    sc.wait_ge(vec.sem, vec.at("fox", "kn", j - 1))
                sc.activation(r_t[:, :], ln_t[:, :], ACT.Exp, scale=-0.5).then_inc(act.step("fox", "r"), 1)

            def fox_vn(j):
                sc.wait_ge(pe.sem, pe.at("fox", "vt", j))
                if not (isinstance(j, int) and j == 0):
                    sc.wait_ge(pe_b.sem, pe_b.at("fox", "o", j - 1))
                sc.activation(vn[:, 0:2, :].rearrange("p a v -> p (a v)"), bank[2][:, 0:256], ACT.Copy
                              ).then_inc(act.step("fox", "vn"), 1)

            def fox_pair(j, first, last):
                if not last:
                    fox_squares(j + 1)
                for qb in range(2):
                    n_k = P * (qb + 1)
                    sc.wait_ge(vec_b.sem, vec_b.at("fox", f"n{qb}", j))
                    if not first:
                        sc.wait_ge(pe_b.sem, pe_b.at("fox", f"t{qb}", j - 1))
                    for e in range(2):
                        sc.activation(pool_a[:, 2 * qb + e, 0:n_k], bank[4 + qb][:, e * n_k:(e + 1) * n_k], ACT.Exp,
                                      bias=small[:, 8 + 2 * qb + e:9 + 2 * qb + e],
                                      accum_out=small[:, 16 + 2 * qb + e:17 + 2 * qb + e]
                                      ).then_inc(act_b.step("fox", f"e{qb}{e}"), 1)
                if not last:
                    fox_rms(j + 1)
                sc.wait_ge(pe_b.sem, pe_b.at("fox", "t0", j))
                sc.activation(xt[:, 0, 0:256], bank[6][:, 0:256], ACT.Copy).then_inc(act_b.step("fox", "pt0"), 1)
                sc.wait_ge(pe_b.sem, pe_b.at("fox", "t1", j))
                sc.activation(silu_t[:, :, 0:256], bank[7][:, :].rearrange("p (a b) -> p a b", a=2), ACT.Copy
                              ).then_inc(act_b.step("fox", "pt1"), 1)
                if not last:
                    fox_vn(j + 1)

            fox_squares(0)
            fox_rms(0)
            fox_vn(0)
            one_behind(sc, 8, fox_pair)
            out2("oout")

        @block.vector
        def _(ve):
            def split_lo(stage, i, s):
                n = W11 if wide(stage) else W8
                q = FIRST_QUAD[stage] + i
                ve.wait_ge(w_hi_ready, SLOTS * q + s + 1)
                ve.tensor_tensor(w_lo[:, s, 0:n], raw[:, s, 0:n], w_hi[:, s, 0:n].bitcast(F32), ALU.subtract
                                 ).then_inc(w_lo_ready, 1)

            def split_next(stage, i, s):
                if isinstance(i, int) and i == QUADS[stage] - 1:
                    nxt = stage_after(stage)
                    if nxt:
                        split_lo(nxt, 0, s)
                else:
                    split_lo(stage, i + 1, s)

            def quads(stage, body):
                body(0)
                if QUADS[stage] > 2:
                    with ve.Fori(1, QUADS[stage] - 1) as i:
                        body(i)
                body(QUADS[stage] - 1)

            def own(phase, step, i=0):
                ve.wait_ge(vec.sem, vec.at(phase, step, i))

            def pre(phase):
                ts = tok(phase)
                n = ts.stop - ts.start
                l = {"pree": 0, "preo": 1}.get(phase)
                if l is not None:
                    ve.scalar_tensor_tensor(gs[:, l, :], mod[:, l, 1, :], 1.0, par("norm_g", 8 * l, 8), ALU.add, ALU.mult
                                            ).then_inc(vec.step(phase, "gs"), 1)
                    own(phase, "gs")
                ve.wait_ge(act.sem, act.at(phase, "r"))
                for what, c in lagged("t", "lo"):
                    if what == "t":
                        if c >= 2:
                            own(phase, f"lo{c - 2}")
                        g = gain(phase, c) if l is None else gs[:, l, c:c + 1]
                        ve.scalar_tensor_tensor(xt[:, c % 2, 0:n], h[:, c, ts], g, r_t[:, 0:n], ALU.mult, ALU.mult
                                                ).then_inc(vec.step(phase, f"t{c}"), 1)
                    else:
                        ve.wait_ge(act.sem, act.at(phase, f"hi{c}"))
                        if l is None:
                            ve.tensor_tensor(x_lo[:, c, 0:n], xt[:, c % 2, 0:n], x_hi[:, c, 0:n].bitcast(F32),
                                             ALU.subtract).then_inc(vec.step(phase, f"lo{c}"), 1)
                        else:
                            ve.scalar_tensor_tensor(x_lo[:, c, 0:n], xt[:, c % 2, 0:n], mod[:, l, 0, c:c + 1],
                                                    x_hi[:, c, 0:n].bitcast(F32), ALU.add, ALU.subtract
                                                    ).then_inc(vec.step(phase, f"lo{c}"), 1)

            def res(phase):
                ve.wait_ge(act.sem, act.at(phase, "r"))
                for what, c in lagged("t", "h"):
                    if what == "t":
                        if c >= 2:
                            own(phase, f"h{c - 2}")
                        ve.tensor_tensor(xt[:, c % 2, :], f[:, c, :], r_t[:, 0:T], ALU.mult
                                         ).then_inc(vec.step(phase, f"t{c}"), 1)
                    else:
                        own(phase, f"t{c}")
                        ve.scalar_tensor_tensor(h[:, c, :], xt[:, c % 2, :], gain(phase, c), h[:, c, :],
                                                ALU.mult, ALU.add).then_inc(vec.step(phase, f"h{c}"), 1)

            def ffn(k):
                g, d = f"gu{k}", f"dn{k}"
                pre(f"pre{k}")

                def ada(phase, i, it):
                    ve.wait_ge(ada_in, 16 * (12 * k + i) + 16)
                    ve.tensor_tensor(ada_raw[:, :, :], ada_raw[:, :, :], cond[:, :].unsqueeze(2).broadcast_to([P, DC, P]),
                                     ALU.mult).then_inc(vec.step(phase, "am"), 1)
                    own(phase, "am", it)
                    if not (isinstance(i, int) and i == 0 and k == 0):
                        if isinstance(i, int) and i == 0:
                            ve.wait_ge(pe.sem, pe.at(f"dn{k - 1}", "ada"))
                        else:
                            ve.wait_ge(pe.sem, pe.at(g, "ada", i - 1))
                    ve.reduce_sum(ada_sum, ada_raw[:, :, :].rearrange("p k n -> p n k"), AX.X
                                  ).then_inc(vec.step(phase, "ar"), 1)

                def gu_quad(i):
                    q = FIRST_QUAD[g] + i
                    ada(g, i, i)
                    for p in range(2):
                        j = 2 * i + p
                        ve.wait_ge(act.sem, act.at(g, f"silu{p}", i))
                        ve.wait_ge(unit_done, SLOTS * q + 2 * p + 2)
                        hi = a_hi[:, bass.ds(j, 1), :].rearrange("p a t -> p (a t)")
                        lo = a_lo[:, bass.ds(j, 1), :].rearrange("p a t -> p (a t)")
                        ve.tensor_tensor(hi, silu_t[:, p, :], bank[2 * p + 1][:, 0:T], ALU.mult
                                         ).then_inc(vec.step(g, f"hi{p}"), 1)
                        own(g, f"lo{p}", i - 1)
                        ve.tensor_tensor(xt[:, p, :], silu_t[:, p, :], bank[2 * p + 1][:, 0:T], ALU.mult
                                         ).then_inc(vec.step(g, f"full{p}"), 1)
                        split_next(g, i, 2 * p)
                        own(g, f"full{p}", i)
                        ve.tensor_tensor(lo, xt[:, p, :], hi.bitcast(F32), ALU.subtract).then_inc(vec.step(g, f"lo{p}"), 1)
                        split_next(g, i, 2 * p + 1)

                quads(g, gu_quad)

                def dn_quad(i):
                    for s in range(SLOTS):
                        split_next(d, i, s)
                    if isinstance(i, int) and i == 0:
                        ada(d, 11, 0)

                quads(d, dn_quad)
                ve.wait_ge(pe.sem, pe.at(d, "ada"))
                flat = mod[:, :, :, :].rearrange("p l a c -> p (l a c)")
                ve.tensor_tensor(flat[:, 12 * k:12 * k + 12], ADA[:, 0:12], par("ada_b", 12 * k, 12), ALU.add
                                 ).then_inc(vec.step(d, "mod"), 1)
                res(f"res{k}")

            def evac_quads(stage):
                def quad(i):
                    for s in range(SLOTS):
                        split_next(stage, i, s)
                quads(stage, quad)

            ve.wait_ge(setup_in, 96)
            lam = PARAMS["lam"][0]
            ve.tensor_tensor(lam_pair[:, :], prm[:, lam:lam + 3:2], prm[:, lam + 1:lam + 4:2], ALU.mult
                             ).then_inc(vec.step("setup", "lam"), 1)
            for k, (name, first) in enumerate([("ln_ffn1", 8), ("ln_ffn2", 8), ("ln_ffn1", 24), ("ln_ffn2", 24)]):
                ve.tensor_scalar(half_g[:, k, :], par(name, first, 8), 0.5, None, ALU.mult
                                 ).then_inc(vec.step("setup", f"half{k}"), 1)
            ve.tensor_scalar(sub_g[:, :], par("subln_g"), 1.0 - LAMBDA_INIT, None, ALU.mult).then_inc(vec.step("setup", "subg"), 1)
            ve.tensor_scalar(gq[:, :], par("qnorm_g"), 0.125, None, ALU.mult).then_inc(vec.step("setup", "gq"), 1)
            row = [par("hgrn_lb", 4 * i, 4) for i in range(3)]
            ve.tensor_tensor(lbm[:, :], row[0], row[1], ALU.max).then_inc(vec.step("setup", "lbm"), 1)
            own("setup", "lbm")
            ve.tensor_tensor(lbm[:, :], lbm[:, :], row[2], ALU.max).then_inc(vec.step("setup", "lb0"), 1)
            own("setup", "lb0")
            ve.tensor_tensor(lb3[:, 0, :], row[0], lbm[:, :], ALU.subtract).then_inc(vec.step("setup", "lb1"), 1)
            ve.tensor_tensor(lb3[:, 1:3, :], prm[:, PARAMS["hgrn_lb"][0] + 4:PARAMS["hgrn_lb"][0] + 12].rearrange("p (r c) -> p r c", r=2),
                             lbm[:, :].unsqueeze(1).broadcast_to([P, 2, 4]), ALU.subtract).then_inc(vec.step("setup", "lb2"), 1)
            ve.wait_ge(act.sem, act.at("setup", "lbe"))
            ve.tensor_tensor(lb[:, 0, :], lb3[:, 0, :], lb3[:, 1, :], ALU.add).then_inc(vec.step("setup", "lbs"), 1)
            own("setup", "lbs")
            ve.tensor_tensor(lb[:, 0, :], lb[:, 0, :], lb3[:, 2, :], ALU.add).then_inc(vec.step("setup", "lbt"), 1)
            own("setup", "lbt")
            ve.reciprocal(lb[:, 1, :], lb[:, 0, :]).then_inc(vec.step("setup", "lbr"), 1)
            own("setup", "lbr")
            ve.tensor_tensor(lb[:, 0, :], lb3[:, 0, :], lb[:, 1, :], ALU.mult).then_inc(vec.step("setup", "lbq"), 1)
            own("setup", "lbq")
            ve.tensor_scalar(lb[:, 1, :], lb[:, 0, :], -1.0, 1.0, ALU.mult, ALU.add).then_inc(vec.step("setup", "lbn"), 1)
            ve.wait_ge(act.sem, act.at("setup", "lame"))
            ve.tensor_tensor(neg_lam[:, :], lam_exp[:, 1:2], lam_exp[:, 0:1], ALU.subtract).then_inc(vec.step("setup", "lamd"), 1)
            own("setup", "lamd")
            ve.tensor_scalar(neg_lam[:, :], neg_lam[:, :], -LAMBDA_INIT, None, ALU.add).then_inc(vec.step("setup", "laml"), 1)
            for s in range(SLOTS):
                split_lo("gu0", 0, s)

            ffn(0)
            pre("prec")
            evac_quads("cin")
            ar = arena[:, 0:24 * T]
            c_, x_, b_ = (ar[:, 8 * i * T:8 * (i + 1) * T].rearrange("p (c t) -> p c t", c=DC) for i in range(3))
            ve.wait_ge(act.sem, act.at("cin", "e3", 5))
            ve.tensor_tensor(x_, c_, x_, ALU.mult).then_inc(vec.step("conv", "u"), 1)
            own("conv", "u")
            for c in range(DC):
                ve.tensor_scalar(c_[:, c, :], x_[:, c, :], par("conv_w", 16 + c), None, ALU.mult
                                 ).then_inc(vec.step("conv", f"w2{c}"), 1)
            for back, c in [(b, c) for b in (1, 2) for c in range(DC)]:
                own("conv", f"w{3 - back}{c}")
                ve.scalar_tensor_tensor(c_[:, c, back:T], x_[:, c, 0:T - back], par("conv_w", 8 * (2 - back) + c),
                                        c_[:, c, back:T], ALU.mult, ALU.add).then_inc(vec.step("conv", f"w{2 - back}{c}"), 1)
            own("conv", "w07")
            ve.tensor_tensor(a_hi[:, 0:DC, :], b_, c_, ALU.mult).then_inc(vec.step("conv", "hi"), 1)
            ve.tensor_tensor(x_, b_, c_, ALU.mult).then_inc(vec.step("conv", "full"), 1)
            own("conv", "full")
            ve.tensor_tensor(a_lo[:, 0:DC, :], x_, a_hi[:, 0:DC, :].bitcast(F32), ALU.subtract).then_inc(vec.step("conv", "lo"), 1)
            evac_quads("cout")
            res("resc")
            ffn(1)
            ffn(2)
            pre("prea")
            evac_quads("ain")

            def own_b(phase, step, i):
                ve.wait_ge(vec_b.sem, vec_b.at(phase, step, i))

            def att_rope(hd):
                q_ = arena[:, bass.ds(hd * T, T)]
                k_ = arena[:, bass.ds((8 + hd) * T, T)]
                zero = isinstance(hd, int) and hd == 0
                if not zero:
                    ve.wait_ge(pe_b.sem, pe_b.at("att", "s3", hd - 1))
                ve.tensor_tensor(qs[:, :], q_, con("cos"), ALU.mult).then_inc(vec.step("att", "qc"), 1)
                ve.tensor_tensor(ks[:, :], k_, con("cos"), ALU.mult).then_inc(vec.step("att", "kc"), 1)
                ve.wait_ge(pe.sem, pe.at("att", "pq", hd))
                if not zero:
                    own("att", "ks", hd - 1)
                ve.tensor_tensor(xt[:, 0, :], bank[0][:, 0:T], con("sin"), ALU.mult).then_inc(vec.step("att", "qx"), 1)
                ve.wait_ge(pe.sem, pe.at("att", "pk", hd))
                ve.tensor_tensor(xt[:, 1, :], bank[1][:, 0:T], con("sin"), ALU.mult).then_inc(vec.step("att", "kx"), 1)
                own("att", "qx", hd)
                for c in range(2):
                    ve.tensor_tensor(q_half[64 * c:64 * c + 64, c, :], qs[64 * c:64 * c + 64, :], xt[64 * c:64 * c + 64, 0, :],
                                     ALU.add).then_inc(vec.step("att", f"qs{c}"), 1)
                own("att", "kx", hd)
                ve.tensor_tensor(ks[:, :], ks[:, :], xt[:, 1, :], ALU.add).then_inc(vec.step("att", "ks"), 1)

            def att_head(hd, first, last):
                ve.wait_ge(pe_b.sem, pe_b.at("att", "s0", hd))
                ve.reduce_max(small[:, 0:2], bank[4][:, 0:256].rearrange("p (c k) -> p c k", c=2), AX.X
                              ).then_inc(vec_b.step("att", "m0"), 1)
                own_b("att", "m0", hd)
                ve.tensor_scalar(small[:, 8:10], small[:, 0:2], -0.125, None, ALU.mult).then_inc(vec_b.step("att", "n0"), 1)
                ve.wait_ge(pe_b.sem, pe_b.at("att", "s1", hd))
                ve.reduce_max(small[:, 2:4], bank[5][:, 0:512].rearrange("p (c k) -> p c k", c=2), AX.X
                              ).then_inc(vec_b.step("att", "m1"), 1)
                own_b("att", "m1", hd)
                ve.tensor_scalar(small[:, 10:12], small[:, 2:4], -0.125, None, ALU.mult).then_inc(vec_b.step("att", "n1"), 1)
                for c in range(2):
                    ve.wait_ge(pe_b.sem, pe_b.at("att", f"s{2 + c}", hd))
                    ve.reduce_max(small[0:META, 4 + c:5 + c], bank[6 + c][0:META, 0:T], AX.X
                                  ).then_inc(vec_b.step("att", f"m{2 + c}"), 1)
                own_b("att", "m3", hd)
                ve.tensor_scalar(small[0:META, 12:14], small[0:META, 4:6], -0.125, None, ALU.mult).then_inc(vec_b.step("att", "n2"), 1)
                if not last:
                    att_rope(hd + 1)
                for qb in range(3):
                    n_q = P if qb < 2 else META
                    n_k = P * (qb + 1) if qb < 2 else T
                    e0, e1 = f[0:n_q, 2 * qb, 0:n_k], f[0:n_q, 2 * qb + 1, 0:n_k]
                    r = small[0:n_q, 24 + 2 * qb:26 + 2 * qb]
                    ve.wait_ge(act_b.sem, act_b.at("att", f"e{qb}1", hd))
                    ve.reciprocal(r, small[0:n_q, 16 + 2 * qb:18 + 2 * qb]).then_inc(vec_b.step("att", f"r{qb}"), 1)
                    own_b("att", f"r{qb}", hd)
                    ve.tensor_scalar(r[:, 1:2], r[:, 1:2], neg_lam[0:n_q, :], None, ALU.mult).then_inc(vec_b.step("att", f"l{qb}"), 1)
                    own_b("att", f"l{qb}", hd)
                    ve.tensor_scalar(e1, e1, r[:, 1:2], None, ALU.mult).then_inc(vec_b.step("att", f"b{qb}"), 1)
                    own_b("att", f"b{qb}", hd)
                    ve.scalar_tensor_tensor(e0, e0, r[:, 0:1], e1, ALU.mult, ALU.add).then_inc(vec_b.step("att", f"a{qb}"), 1)
                hi = a_hi[:, bass.ds(hd, 1), :].rearrange("p a t -> p (a t)")
                lo = a_lo[:, bass.ds(hd, 1), :].rearrange("p a t -> p (a t)")
                ve.wait_ge(act_b.sem, act_b.at("att", "r", hd))
                ve.scalar_tensor_tensor(hi, bank[6][:, 0:T], sub_g[:, :], r_t[:, 0:T], ALU.mult, ALU.mult
                                        ).then_inc(vec_b.step("att", "hi"), 1)
                if not first:
                    own_b("att", "lo", hd - 1)
                ve.scalar_tensor_tensor(silu_t[:, 0, :], bank[6][:, 0:T], sub_g[:, :], r_t[:, 0:T], ALU.mult, ALU.mult
                                        ).then_inc(vec_b.step("att", "full"), 1)
                own_b("att", "full", hd)
                ve.tensor_tensor(lo, silu_t[:, 0, :], hi.bitcast(F32), ALU.subtract).then_inc(vec_b.step("att", "lo"), 1)

            ve.wait_ge(act.sem, act.at("ain", "e3", 5))
            att_rope(0)
            one_behind(ve, HEADS, att_head)
            evac_quads("aout")
            res("resa")
            ffn(3)
            pre("pree")
            evac_quads("ein")

            ar2 = arena[:, 0:32 * SEQ]
            q_, f_ = ar2[:, 0:4 * SEQ], ar2[:, 4 * SEQ:8 * SEQ]
            key, qp = ar2[:, 24 * SEQ:28 * SEQ], ar2[:, 28 * SEQ:32 * SEQ]
            st = arena[:, 0:4 * SEQ]
            ve.wait_ge(act.sem, act.at("hg", "sig"))
            for i in range(4):
                ve.tensor_scalar(f_[:, i * SEQ:(i + 1) * SEQ], f_[:, i * SEQ:(i + 1) * SEQ], lb[:, 1, i:i + 1],
                                 lb[:, 0, i:i + 1], ALU.mult, ALU.add).then_inc(vec.step("hg", f"fg{i}"), 1)
            own("hg", "fg3")
            ve.tensor_scalar(key, f_, -1.0, 1.0, ALU.mult, ALU.add).then_inc(vec.step("hg", "key"), 1)
            own("hg", "key")
            ve.tensor_scalar(f_, f_, 1.0, None, ALU.min).then_inc(vec.step("hg", "fm"), 1)
            own("hg", "fm")
            ve.tensor_tensor(qp, q_, f_, ALU.mult).then_inc(vec.step("hg", "q0"), 1)
            ve.wait_ge(pe.sem, pe.at("hg", "dg"))
            own("hg", "q0")
            idb = ident.unsqueeze(1).broadcast_to([P, 4, P])
            for j in range(2):
                ve.tensor_tensor(st[:, j * 512:(j + 1) * 512].rearrange("p (a t) -> p a t", a=4),
                                 bank[j][:, :].rearrange("p (a t) -> p a t", a=4), idb, ALU.mult
                                 ).then_inc(vec.step("hg", f"dg{j}"), 1)
            own("hg", "dg1")
            tot = f_
            tbuf = [ln_t[:, :], sq[:, 0, :]]
            for i in range(LEVELS):
                b = 1 << i
                nb = 64 // b
                ve.wait_ge(pe.sem, pe.at("hg", f"lv{i}"))
                for_all = st.rearrange("p (a n r b) -> p a n r b", a=8, n=nb, r=2, b=b)
                msk = lvl_mask[:, i, :].rearrange("p (n b) -> p n b", n=nb).unsqueeze(1).broadcast_to([P, 8, nb, b])
                ve.copy_predicated(for_all[:, :, :, 1, :], msk,
                                   bank[2 + i % 2][:, :].rearrange("p (a n b) -> p a n b", a=8, n=nb)
                                   ).then_inc(vec.step("hg", f"cp{i}"), 1)
                t3 = tot.rearrange("p (n r) -> p n r", r=2)
                n2 = 1024 // (2 * b)
                qv = qp.rearrange("p (n r b) -> p n r b", r=2, b=b)
                kv = key.rearrange("p (n r b) -> p n r b", r=2, b=b)
                ve.tensor_tensor(qv[:, :, 1, :], qv[:, :, 1, :], t3[:, :, 0].unsqueeze(2).broadcast_to([P, n2, b]), ALU.mult
                                 ).then_inc(vec.step("hg", f"qp{i}"), 1)
                ve.tensor_tensor(kv[:, :, 0, :], kv[:, :, 0, :], t3[:, :, 1].unsqueeze(2).broadcast_to([P, n2, b]), ALU.mult
                                 ).then_inc(vec.step("hg", f"kp{i}"), 1)
                new = tbuf[i % 2][:, 0:n2]
                ve.tensor_tensor(new, t3[:, :, 0], t3[:, :, 1], ALU.mult).then_inc(vec.step("hg", f"tp{i}"), 1)
                own("hg", f"tp{i}")
                tot = new
            sga, sgb = ar2[:, 12 * SEQ:16 * SEQ], ar2[:, 20 * SEQ:24 * SEQ]
            for i in range(8):
                if i < 4:
                    ve.wait_ge(act.sem, act.at("hg", f"r{i}"))
                    src, g, other = bank[i][:, 0:SEQ], par("onorm_g", i), r_t[:, (i % 2) * SEQ:(i % 2 + 1) * SEQ]
                    gate = sga[:, i * SEQ:(i + 1) * SEQ]
                else:
                    ve.wait_ge(pe.sem, pe.at("hg", f"pl{i - 4}"))
                    src, g = bank[6 + i % 2][:, 0:SEQ], par("pool_scale", i - 4)
                    other = gate = sgb[:, (i - 4) * SEQ:(i - 3) * SEQ]
                t0, t1 = (f_[:, (2 * b + i % 2) * SEQ:(2 * b + i % 2 + 1) * SEQ] for b in range(2))
                if i == 0:
                    own("hg", f"tp{LEVELS - 1}")
                if i >= 2:
                    own("hg", f"lo{i - 2}")
                ve.scalar_tensor_tensor(t0, src, g, other, ALU.mult, ALU.mult).then_inc(vec.step("hg", f"on{i}"), 1)
                own("hg", f"on{i}")
                if i < 4:
                    ve.tensor_tensor(a_hi[:, i, 0:SEQ], t0, gate, ALU.mult).then_inc(vec.step("hg", f"hi{i}"), 1)
                    ve.tensor_tensor(t1, t0, gate, ALU.mult).then_inc(vec.step("hg", f"full{i}"), 1)
                else:
                    ve.tensor_copy(a_hi[:, i, 0:SEQ], t0).then_inc(vec.step("hg", f"hi{i}"), 1)
                    ve.tensor_copy(t1, t0).then_inc(vec.step("hg", f"full{i}"), 1)
                own("hg", f"full{i}")
                ve.tensor_tensor(a_lo[:, i, 0:SEQ], t1, a_hi[:, i, 0:SEQ].bitcast(F32), ALU.subtract
                                 ).then_inc(vec.step("hg", f"lo{i}"), 1)

            def out2(stage, l):
                for i in range(2):
                    q = FIRST_QUAD[stage] + i
                    for s in range(SLOTS):
                        split_next(stage, i, s)
                        c = SLOTS * i + s
                        ve.wait_ge(unit_done, SLOTS * q + s + 1)
                        ve.scalar_tensor_tensor(h[:, c, META:T], bank[s][:, 0:SEQ], mod[:, l, 2, c:c + 1],
                                                h[:, c, META:T], ALU.mult, ALU.add).then_inc(vec.step(stage, f"h{s}"), 1)

            out2("eout", 0)
            pre("preo")
            evac_quads("oin")

            ve.wait_ge(act.sem, act.at("fl", "whi"))
            ve.tensor_tensor(flw_lo[:, :, :], flw[:, :, :], flw_hi[:, :, :].bitcast(F32), ALU.subtract).then_inc(vec.step("fl", "wlo"), 1)
            z, nz, az = (pool_a[0:16, i, :] for i in range(3))
            ls, cum, ncum = (pool_b[0:16, i, :] for i in (1, 0, 3))
            ve.wait_ge(pe.sem, pe.at("fl", "tr"))
            ve.tensor_scalar(z, bank[2][0:16, 0:SEQ], par("b_f")[0:16, :], None, ALU.add).then_inc(vec.step("fl", "z"), 1)
            own("fl", "z")
            ve.tensor_scalar(nz, z, -1.0, None, ALU.mult).then_inc(vec.step("fl", "nz"), 1)
            own("fl", "nz")
            ve.tensor_tensor(az, z, nz, ALU.max).then_inc(vec.step("fl", "az"), 1)
            ve.wait_ge(act.sem, act.at("fl", "ln"))
            ve.scalar_tensor_tensor(ls, z, 0.0, pool_b[0:16, 0, :], ALU.min, ALU.subtract).then_inc(vec.step("fl", "logf"), 1)
            own("fl", "logf")
            ones2 = ones[0:16, 0:1].broadcast_to([16, SEQ])
            ve.tensor_tensor_scan(cum, ones2, ls, 0.0, ALU.mult, ALU.add
                                  ).then_inc(vec.step("fl", "cum"), 1)
            own("fl", "cum")
            ve.tensor_scalar(ncum, cum, -1.0, None, ALU.mult).then_inc(vec.step("fl", "ncum"), 1)
            own("fl", "ncum")

            def fox_norm(j):
                ve.wait_ge(act.sem, act.at("fox", "r", j))
                if not (isinstance(j, int) and j == 0):
                    ve.wait_ge(pe_b.sem, pe_b.at("fox", "s1", j - 1))
                for e in range(2):
                    ps = slice(64 * e, 64 * e + 64)
                    ve.scalar_tensor_tensor(q_half[ps, e, 0:SEQ], ar2[ps, bass.ds(j * SEQ, SEQ)], gq[ps, :], r_t[ps, 0:SEQ],
                                            ALU.mult, ALU.mult).then_inc(vec.step("fox", f"qn{e}"), 1)
                ve.scalar_tensor_tensor(ks[:, 0:SEQ], ar2[:, bass.ds((8 + j) * SEQ, SEQ)], par("knorm_g"), r_t[:, SEQ:512],
                                        ALU.mult, ALU.mult).then_inc(vec.step("fox", "kn"), 1)
                pick = CONSTS["pick"][0]
                for e in range(2):
                    ve.tensor_scalar(lnb[0:16, e, :], ncum, cst[0:16, bass.ds(pick + 2 * j + e, 1)], None, ALU.mult
                                     ).then_inc(vec.step("fox", f"d{e}"), 1)

            def fox_pair(j, first, last):
                for qb in range(2):
                    n_k = P * (qb + 1)
                    ve.wait_ge(pe_b.sem, pe_b.at("fox", f"s{qb}", j))
                    ve.reduce_max(small[:, 2 * qb:2 * qb + 2], bank[4 + qb][:, 0:2 * n_k].rearrange("p (e k) -> p e k", e=2),
                                  AX.X).then_inc(vec_b.step("fox", f"m{qb}"), 1)
                    own_b("fox", f"m{qb}", j)
                    ve.tensor_scalar(small[:, 8 + 2 * qb:10 + 2 * qb], small[:, 2 * qb:2 * qb + 2], -1.0, None, ALU.mult
                                     ).then_inc(vec_b.step("fox", f"n{qb}"), 1)
                for qb in range(2):
                    n_k = P * (qb + 1)
                    ve.wait_ge(act_b.sem, act_b.at("fox", f"e{qb}1", j))
                    ve.reciprocal(small[:, 24 + 2 * qb:26 + 2 * qb], small[:, 16 + 2 * qb:18 + 2 * qb]
                                  ).then_inc(vec_b.step("fox", f"r{qb}"), 1)
                    own_b("fox", f"r{qb}", j)
                    for e in range(2):
                        ve.tensor_scalar(pool_a[:, 2 * qb + e, 0:n_k], pool_a[:, 2 * qb + e, 0:n_k],
                                         small[:, 24 + 2 * qb + e:25 + 2 * qb + e], None, ALU.mult
                                         ).then_inc(vec_b.step("fox", f"p{qb}{e}"), 1)
                if not last:
                    fox_norm(j + 1)
                hi = a_hi[:, bass.ds(j, 1), 0:SEQ].rearrange("p a t -> p (a t)")
                lo = a_lo[:, bass.ds(j, 1), 0:SEQ].rearrange("p a t -> p (a t)")
                gate = ar2[:, bass.ds((24 + j) * SEQ, SEQ)]
                ve.wait_ge(act.sem, act.at("fl", "sg"))
                ve.wait_ge(pe_b.sem, pe_b.at("fox", "o", j))
                ve.tensor_tensor(hi, bank[3][:, 0:SEQ], gate, ALU.mult).then_inc(vec_b.step("fox", "hi"), 1)
                if not first:
                    own_b("fox", "lo", j - 1)
                ve.tensor_tensor(xt[:, 1, 0:SEQ], bank[3][:, 0:SEQ], gate, ALU.mult).then_inc(vec_b.step("fox", "full"), 1)
                own_b("fox", "full", j)
                ve.tensor_tensor(lo, xt[:, 1, 0:SEQ], hi.bitcast(F32), ALU.subtract).then_inc(vec_b.step("fox", "lo"), 1)

            fox_norm(0)
            one_behind(ve, 8, fox_pair)
            out2("oout", 1)

        @block.gpsimd
        def _(gp):
            gp.memset(ones[:, :], 1.0).then_inc(pool.step("setup", "ones"), 1)
            gp.memset(eps6[:, :], 1e-6).then_inc(pool.step("setup", "eps6"), 1)
            gp.memset(eps5[:, :], 1e-5).then_inc(pool.step("setup", "eps5"), 1)
            gp.memset(one[:, :], 1.0).then_inc(pool.step("setup", "one"), 1)
            gp.memset(q_half[:, :, :], 0.0).then_inc(pool.step("setup", "q_half"), 1)

            def zero(phase, prev):
                if prev:
                    gp.wait_ge(pe.sem, pe.at(*prev))
                gp.memset(sq_sum[:, :], 0.0).then_inc(pool.step(phase, "zero"), 1)
                gp.wait_ge(pool.sem, pool.at(phase, "zero"))

            def ffn_sums(k, prev):
                d = f"dn{k}"
                zero(d, prev)

                def add(i, p, phase, j):
                    gp.wait_ge(act.sem, act.at(d, f"sq{p}", i))
                    gp.tensor_tensor(sq_sum[:, :], sq_sum[:, :], sq[:, p, :], ALU.add).then_inc(pool.step(phase, f"add{p}"), 1)
                    gp.wait_ge(pool.sem, pool.at(phase, f"add{p}", j))
                with gp.Fori(0, 3) as i:
                    for p in range(2):
                        add(i, p, d + "s", i)
                add(3, 0, d + "t", 0)

            def out1(stage, prev):
                zero(stage, prev)
                for o in range(7):
                    gp.wait_ge(act.sem, act.at(stage, f"sq{o % 4}", o // 4))
                    gp.tensor_tensor(sq_sum[:, :], sq_sum[:, :], sq[:, o % 2, :], ALU.add).then_inc(pool.step(stage, f"add{o}"), 1)
                    gp.wait_ge(pool.sem, pool.at(stage, f"add{o}"))

            ffn_sums(0, None)
            out1("cout", ("res0", "ss"))
            ffn_sums(1, ("resc", "ss"))
            ffn_sums(2, ("res1", "ss"))
            out1("aout", ("res2", "ss"))
            ffn_sums(3, ("resa", "ss"))

            ar = arena[:, 0:32 * SEQ]
            u = ar[:, 16 * SEQ:20 * SEQ].rearrange("p (g t) -> p g t", g=4)
            bufs = [pool_a[:, :, :], pool_b[:, :, :]]
            gp.wait_ge(act.sem, act.at("ein", "e3", 5))
            src = u
            for lvl in range(4):
                d = 1 << lvl
                dst = bufs[lvl % 2]
                gp.tensor_copy(dst[:, lvl:4, 0:d], src[:, lvl:4, 0:d]).then_inc(pool.step("hg", f"c{lvl}"), 1)
                gp.tensor_tensor(dst[:, lvl:4, d:SEQ], src[:, lvl:4, d:SEQ], src[:, lvl:4, 0:SEQ - d], ALU.add
                                 ).then_inc(pool.step("hg", f"s{lvl}"), 1)
                gp.wait_ge(pool.sem, pool.at("hg", f"s{lvl}"))
                src = dst
            inv = CONSTS["invcount"][0]
            for g in range(4):
                gp.tensor_tensor(bufs[g % 2][:, g, 0:16], bufs[g % 2][:, g, 0:16], cst[:, inv + 16 * g:inv + 16 * g + 16],
                                 ALU.mult).then_inc(pool.step("hg", f"i{g}"), 1)
            for g in range(4):
                gp.tensor_scalar(bufs[g % 2][:, g, 16:SEQ], bufs[g % 2][:, g, 16:SEQ], 1.0 / (2 << g), None, ALU.mult
                                 ).then_inc(pool.step("hg", f"j{g}"), 1)
            gp.wait_ge(pool.sem, pool.at("hg", "j3"))
            for g in range(4):
                gp.tensor_tensor(bufs[g % 2][:, g, :], bufs[g % 2][:, g, :], u[:, g, :], ALU.subtract
                                 ).then_inc(pool.step("hg", f"p{g}"), 1)

        @block.tensor
        def _(te):
            def product(dst, s, w, rhs_hi, rhs_lo, first, last):
                a = w * P
                te.matmul(dst, w_hi[:, s, a:a + P], rhs_hi, start=first, stop=False)
                te.matmul(dst, w_hi[:, s, a:a + P], rhs_lo, start=False, stop=False)
                return te.matmul(dst, w_lo[:, s, a:a + P], rhs_hi, start=False, stop=last)

            def quads(stage, body):
                body(0)
                with te.Fori(1, QUADS[stage]) as i:
                    body(i)

            def project(stage, n, src_hi, src_lo, free, after=None, k_ready=None, extra=None):
                def quad(i):
                    q = FIRST_QUAD[stage] + i
                    for s in range(SLOTS):
                        te.wait_ge(w_lo_ready, SLOTS * q + s + 1)
                        if isinstance(i, int) and i == 0:
                            if s == 0 and after:
                                te.wait_ge(*after)
                        else:
                            te.wait_ge(*free(s, i - 1))
                        for k in range(DC):
                            if isinstance(i, int) and i == 0 and s == 0 and k_ready:
                                te.wait_ge(*k_ready(k))
                            last = product(bank[s][:, 0:n], s, k, src_hi[:, k, 0:n], src_lo[:, k, 0:n],
                                           k == 0, k == DC - 1)
                        last.then_inc(unit_done, 1)
                    if extra:
                        extra(i)
                quads(stage, quad)

            def pre(phase):
                n = tok(phase).stop - tok(phase).start
                for c in range(DC):
                    te.wait_ge(act.sem, act.at(phase, f"sq{c}"))
                    te.matmul(STAT[:, 0:n], ones[:, :], sq[:, c % 2, 0:n], start=(c == 0), stop=(c == DC - 1)
                              ).then_inc(pe.step(phase, f"ss{c}"), 1)

            def lo_ready(phase):
                return lambda k: (vec.sem, vec.at(phase, f"lo{k}"))

            def ada(k, i):
                if isinstance(i, int) and i == 11:
                    te.wait_ge(vec.sem, vec.at(f"dn{k}", "ar"))
                else:
                    te.wait_ge(vec.sem, vec.at(f"gu{k}", "ar", i))
                if k and isinstance(i, int) and i == 0:
                    te.wait_ge(vec.sem, vec.at(f"dn{k - 1}", "mod"))
                return te.matmul(ADA[:, bass.ds(i, 1)], ada_sum, ones[:, 0:1], start=True, stop=True)

            def res(phase, last_add, last_sq):
                te.wait_ge(pool.sem, last_add)
                te.matmul(STAT[:, 0:T], ones[:, :], sq_sum[:, :], start=True, stop=False)
                te.wait_ge(act.sem, last_sq)
                te.matmul(STAT[:, 0:T], ones[:, :], sq[:, 1, :], start=False, stop=True).then_inc(pe.step(phase, "ss"), 1)

            def ffn(k):
                g, d = f"gu{k}", f"dn{k}"
                pre(f"pre{k}")
                project(g, T, x_hi, x_lo, lambda s, i: (vec.sem, vec.at(g, f"full{s // 2}", i)),
                        k_ready=lo_ready(f"pre{k}"),
                        extra=lambda i: ada(k, i).then_inc(pe.step(g, "ada"), 1))

                def dn_quad(i):
                    q = FIRST_QUAD[d] + i
                    for s in range(SLOTS):
                        te.wait_ge(w_lo_ready, SLOTS * q + s + 1)
                        p = s // 2
                        if isinstance(i, int) and i == 0:
                            if s == 0:
                                te.wait_ge(vec.sem, vec.at(g, "lo0", 10))
                            if s == 1:
                                te.wait_ge(vec.sem, vec.at(g, "lo1", 10))
                        elif s % 2 == 0:
                            te.wait_ge(act.sem, act.at(d, f"sq{p}", i - 1))
                        for kk in range(HALF):
                            kc = HALF * (s % 2) + kk
                            last = product(bank[2 * p][:, 0:T], s, kk, a_hi[:, kc, :], a_lo[:, kc, :],
                                           kc == 0, kc == FC - 1)
                        last.then_inc(unit_done, 1)
                quads(d, dn_quad)
                ada(k, 11).then_inc(pe.step(d, "ada"), 1)
                res(f"res{k}", pool.at(d + "t", "add0"), act.at(d, "sq1", 3))

            def evac_free(stage):
                return lambda s, i: (act.sem, act.at(stage, f"e{s}", i))

            def out1(stage, res_, ready):
                project(stage, T, a_hi, a_lo, lambda s, i: (act.sem, act.at(stage, f"sq{s}", i)), after=ready)
                res(res_, pool.at(stage, "add6"), act.at(stage, "sq3", 1))

            te.wait_ge(pool.sem, pool.at("setup", "ones"))
            te.wait_ge(vec.sem, vec.at("setup", "lam"))
            te.matmul(bank[7][:, 0:2], ones[:, :], lam_pair[:, :], start=True, stop=True).then_inc(pe.step("setup", "lams"), 1)
            te.wait_ge(act.sem, act.at("setup", "cond"))

            ffn(0)
            pre("prec")
            project("cin", T, x_hi, x_lo, evac_free("cin"), k_ready=lo_ready("prec"))
            out1("cout", "resc", (vec.sem, vec.at("conv", "lo")))
            ffn(1)
            ffn(2)
            pre("prea")
            project("ain", T, x_hi, x_lo, evac_free("ain"), k_ready=lo_ready("prea"))

            def att_swap(hd):
                if not (isinstance(hd, int) and hd == 0):
                    te.wait_ge(vec.sem, vec.at("att", "kx", hd - 1))
                te.matmul(bank[0][:, 0:T], con("ropeswap"), arena[:, bass.ds(hd * T, T)], start=True, stop=True
                          ).then_inc(pe.step("att", "pq"), 1)
                te.matmul(bank[1][:, 0:T], con("ropeswap"), arena[:, bass.ds((8 + hd) * T, T)], start=True, stop=True
                          ).then_inc(pe.step("att", "pk"), 1)
                te.wait_ge(act.sem, act.at("att", "vs", hd))
                te.transpose(bank[2][:, 0:P], vs[:, 0:P], ident)
                te.transpose(bank[2][:, P:2 * P], vs[:, P:2 * P], ident)
                te.transpose(bank[2][0:META, 2 * P:3 * P], vs[:, 256:T], ident).then_inc(pe.step("att", "vt"), 1)

            def att_head(hd, first, last_one):
                te.wait_ge(vec.sem, vec.at("att", "ks", hd))
                if not first:
                    te.wait_ge(act_b.sem, act_b.at("att", "at3", hd - 1))
                for qb in range(3):
                    q0 = P * qb
                    n_q = P if qb < 2 else META
                    n_k = P * (qb + 1) if qb < 2 else T
                    if qb == 2 and not first:
                        te.wait_ge(vec_b.sem, vec_b.at("att", "full", hd - 1))
                    for c in range(2):
                        dst = (bank[4][:, c * P:(c + 1) * P], bank[5][:, c * 256:(c + 1) * 256],
                               bank[6 + c][:, 0:T])[qb]
                        te.matmul(dst[0:n_q, :], q_half[:, c, q0:q0 + n_q], ks[:, 0:n_k], start=True, stop=False)
                        last = te.matmul(dst[0:n_q, q0:q0 + n_q], ident[0:n_q, 0:n_q], con("causal")[0:n_q, 0:n_q],
                                         start=False, stop=True)
                        if qb == 2:
                            last.then_inc(pe_b.step("att", f"s{2 + c}"), 1)
                    if qb < 2:
                        last.then_inc(pe_b.step("att", f"s{qb}"), 1)
                if not last_one:
                    att_swap(hd + 1)
                te.wait_ge(vec_b.sem, vec_b.at("att", "a0", hd))
                te.transpose(bank[3][:, 0:P], f[:, 0, 0:P], ident).then_inc(pe_b.step("att", "t0"), 1)
                te.wait_ge(vec_b.sem, vec_b.at("att", "a1", hd))
                te.transpose(bank[4][:, 0:P], f[:, 2, 0:P], ident)
                te.transpose(bank[4][:, P:2 * P], f[:, 2, P:2 * P], ident).then_inc(pe_b.step("att", "t1"), 1)
                te.wait_ge(vec_b.sem, vec_b.at("att", "a2", hd))
                te.matmul(bank[5][:, 0:16], f[0:META, 4, 0:P], ident[0:META, 0:META], start=True, stop=True)
                te.matmul(bank[5][:, 16:32], f[0:META, 4, P:2 * P], ident[0:META, 0:META], start=True, stop=True)
                te.matmul(bank[5][0:META, 32:48], f[0:META, 4, 256:T], ident[0:META, 0:META], start=True, stop=True
                          ).then_inc(pe_b.step("att", "t2"), 1)
                at_ = f[:, 6:8, :]
                te.wait_ge(act_b.sem, act_b.at("att", "at3", hd))
                te.wait_ge(act.sem, act.at("att", "vn2", hd))
                te.matmul(bank[6][:, 0:T], vn[:, 0, :], at_[:, 0, :], start=True, stop=False)
                te.matmul(bank[6][:, P:T], vn[:, 1, :], at_[:, 1, P:T], start=False, stop=False)
                te.matmul(bank[6][:, 256:T], vn[0:META, 2, :], at2[:, :], start=False, stop=True
                          ).then_inc(pe_b.step("att", "o"), 1)
                te.wait_ge(act_b.sem, act_b.at("att", "osq", hd))
                te.matmul(bank[7][:, 0:T], ones[:, :], sq[:, 0, :], start=True, stop=True).then_inc(pe_b.step("att", "oss"), 1)

            te.wait_ge(act.sem, act.at("ain", "e3", 5))
            att_swap(0)
            one_behind(te, HEADS, att_head)
            out1("aout", "resa", (vec_b.sem, vec_b.at("att", "lo", HEADS - 1)))
            ffn(3)
            pre("pree")
            project("ein", SEQ, x_hi, x_lo, evac_free("ein"), k_ready=lo_ready("pree"))

            ar = arena[:, 0:32 * SEQ]
            te.wait_ge(act.sem, act.at("ein", "e3", 5))
            for j in range(2):
                for a in range(4):
                    g = 4 * j + a
                    last = te.transpose(bank[6 + j][:, a * P:(a + 1) * P], ar[:, 8 * SEQ + g * P:8 * SEQ + (g + 1) * P], ident)
                last.then_inc(pe.step("hg", f"vt{j}"), 1)
            key, qp, q_ = ar[:, 24 * SEQ:28 * SEQ], ar[:, 28 * SEQ:32 * SEQ], ar[:, 0:4 * SEQ]
            te.wait_ge(vec.sem, vec.at("hg", "key"))
            for g in range(8):
                last = te.matmul(bank[g // 4][:, (g % 4) * P:(g % 4 + 1) * P], key[:, g * P:(g + 1) * P],
                                 q_[:, g * P:(g + 1) * P], start=True, stop=True)
            last.then_inc(pe.step("hg", "dg"), 1)
            for i in range(LEVELS):
                b = 1 << i
                if i == 0:
                    te.wait_ge(vec.sem, vec.at("hg", "q0"))
                else:
                    te.wait_ge(vec.sem, vec.at("hg", f"kp{i - 1}"))
                qv = qp.rearrange("p (g n r b) -> p g n r b", g=8, r=2, b=b)
                for g in range(8):
                    last = te.matmul(bank[2 + i % 2][:, g * 64:(g + 1) * 64], key[:, g * P:(g + 1) * P],
                                     qv[:, g, :, 1, :], start=True, stop=True)
                last.then_inc(pe.step("hg", f"lv{i}"), 1)
            te.wait_ge(vec.sem, vec.at("hg", f"kp{LEVELS - 1}"))
            te.wait_ge(act.sem, act.at("hg", "vn1"))
            for a in range(4):
                last = te.matmul(bank[6][:, a * P:(a + 1) * P], key[:, 2 * a * P:(2 * a + 1) * P],
                                 qp[:, (2 * a + 1) * P:(2 * a + 2) * P], start=True, stop=True)
            last.then_inc(pe.step("hg", f"lv{LEVELS}"), 1)
            i_tok = ar[:, 8 * SEQ:12 * SEQ]
            st = ar[:, 0:4 * SEQ]
            te.wait_ge(act.sem, act.at("hg", "s2"))
            te.wait_ge(vec.sem, vec.at("hg", f"cp{LEVELS - 1}"))
            for a in range(4):
                v0, v1 = i_tok[:, 2 * a * P:(2 * a + 1) * P], i_tok[:, (2 * a + 1) * P:(2 * a + 2) * P]
                te.matmul(bank[a][:, 0:P], v0, st[:, 2 * a * P:(2 * a + 1) * P], start=True, stop=True)
                te.matmul(bank[a][:, P:2 * P], v0, xt[:, a // 2, (a % 2) * P:(a % 2 + 1) * P], start=True, stop=False)
                te.matmul(bank[a][:, P:2 * P], v1, st[:, (2 * a + 1) * P:(2 * a + 2) * P], start=False, stop=True
                          ).then_inc(pe.step("hg", f"pv{a}"), 1)
            for a in range(4):
                te.wait_ge(act.sem, act.at("hg", f"sq{a}"))
                if a >= 2:
                    te.wait_ge(act.sem, act.at("hg", f"ln{a - 2}"))
                te.matmul(bank[4 + a % 2][:, 0:SEQ], ones[:, :], silu_t[:, a % 2, 0:SEQ], start=True, stop=True
                          ).then_inc(pe.step("hg", f"ss{a}"), 1)
            for g in range(4):
                te.wait_ge(pool.sem, pool.at("hg", f"p{g}"))
                if g >= 2:
                    te.wait_ge(vec.sem, vec.at("hg", f"on{g + 2}"))
                te.matmul(bank[6 + g % 2][:, 0:SEQ], poolw[:, g, :], (pool_a, pool_b)[g % 2][:, g, :], start=True, stop=True
                          ).then_inc(pe.step("hg", f"pl{g}"), 1)

            project("eout", SEQ, a_hi, a_lo, lambda s, i: (vec.sem, vec.at("eout", f"h{s}", i)),
                    after=(vec.sem, vec.at("hg", "lo7")))
            pre("preo")
            project("oin", SEQ, x_hi, x_lo, evac_free("oin"), k_ready=lo_ready("preo"))

            te.wait_ge(vec.sem, vec.at("fl", "wlo"))
            te.wait_ge(act.sem, act.at("oin", "e3", 7))
            for j in range(2):
                for k in range(DC):
                    ts = slice(j * P, (j + 1) * P)
                    te.matmul(bank[j][:, 0:16], x_hi[:, k, ts], flw_hi[:, k, :], start=(k == 0), stop=False)
                    te.matmul(bank[j][:, 0:16], x_hi[:, k, ts], flw_lo[:, k, :], start=False, stop=False)
                    last = te.matmul(bank[j][:, 0:16], x_lo[:, k, ts], flw_hi[:, k, :], start=False, stop=(k == DC - 1))
            last.then_inc(pe.step("fl", "fl"), 1)
            te.wait_ge(act.sem, act.at("fl", "cp1"))
            te.transpose(bank[2][0:16, 0:P], small[:, 0:16], ident)
            te.transpose(bank[2][0:16, P:2 * P], small[:, 16:32], ident).then_inc(pe.step("fl", "tr"), 1)

            def fox_sums(j):
                te.wait_ge(act.sem, act.at("fox", "sqq", j))
                if not (isinstance(j, int) and j == 0):
                    te.wait_ge(act.sem, act.at("fox", "ln", j - 1))
                te.matmul(bank[0][:, 0:SEQ], con("ones64"), sq[:, 0, 0:SEQ], start=True, stop=True).then_inc(pe.step("fox", "nq"), 1)
                te.wait_ge(act.sem, act.at("fox", "sqk", j))
                te.matmul(bank[0][:, SEQ:512], con("ones64"), sq[:, 1, 0:SEQ], start=True, stop=True).then_inc(pe.step("fox", "nk"), 1)
                te.wait_ge(act.sem, act.at("fox", "vs", j))
                te.transpose(bank[2][:, 0:P], vs[:, 0:P], ident)
                te.transpose(bank[2][:, P:2 * P], vs[:, P:2 * P], ident).then_inc(pe.step("fox", "vt"), 1)

            def fox_pair(j, first, last_one):
                te.wait_ge(vec.sem, vec.at("fox", "d1", j))
                if not first:
                    te.wait_ge(act_b.sem, act_b.at("fox", "e11", j - 1))
                for qb in range(2):
                    n_k = P * (qb + 1)
                    for e in range(2):
                        dst = bank[4 + qb][:, e * n_k:(e + 1) * n_k]
                        te.matmul(dst, ones[0:16, :], lnb[0:16, e, 0:n_k], start=True, stop=False)
                        te.matmul(dst, q_half[:, e, qb * P:(qb + 1) * P], ks[:, 0:n_k], start=False, stop=False)
                        last = te.matmul(dst[:, qb * P:n_k], ident, con("causal"), start=False, stop=True)
                    last.then_inc(pe_b.step("fox", f"s{qb}"), 1)
                if not last_one:
                    fox_sums(j + 1)
                if not first:
                    te.wait_ge(act_b.sem, act_b.at("fox", "pt1", j - 1))
                te.wait_ge(vec_b.sem, vec_b.at("fox", "p01", j))
                te.transpose(bank[6][:, 0:P], pool_a[:, 0, 0:P], ident)
                te.transpose(bank[6][:, P:2 * P], pool_a[:, 1, 0:P], ident).then_inc(pe_b.step("fox", "t0"), 1)
                te.wait_ge(vec_b.sem, vec_b.at("fox", "p11", j))
                for e in range(2):
                    for kb in range(2):
                        last = te.transpose(bank[7][:, (2 * e + kb) * P:(2 * e + kb + 1) * P],
                                            pool_a[:, 2 + e, kb * P:(kb + 1) * P], ident)
                last.then_inc(pe_b.step("fox", "t1"), 1)
                te.wait_ge(act_b.sem, act_b.at("fox", "pt1", j))
                te.wait_ge(act.sem, act.at("fox", "vn", j))
                if not first:
                    te.wait_ge(vec_b.sem, vec_b.at("fox", "full", j - 1))
                for e in range(2):
                    ps = slice(64 * e, 64 * e + 64)
                    te.matmul(bank[3][ps, 0:P], vn[:, 0, ps], xt[:, 0, e * P:(e + 1) * P], start=True, stop=True)
                    te.matmul(bank[3][ps, P:2 * P], vn[:, 0, ps], silu_t[:, e, 0:P], start=True, stop=False)
                    last = te.matmul(bank[3][ps, P:2 * P], vn[:, 1, ps], silu_t[:, e, P:2 * P], start=False, stop=True)
                last.then_inc(pe_b.step("fox", "o"), 1)

            te.wait_ge(vec.sem, vec.at("fl", "z"))
            fox_sums(0)
            one_behind(te, 8, fox_pair)
            project("oout", SEQ, a_hi, a_lo, lambda s, i: (vec.sem, vec.at("oout", f"h{s}", i)),
                    after=(vec_b.sem, vec_b.at("fox", "lo", 7)))


def unit_tiles(w):
    k, n = w.shape
    return w.reshape(k // P, P, n // P, P).transpose(2, 1, 0, 3).reshape(n // P, P, (k // P) * P)


def interleave(*groups):
    return np.stack(groups, axis=1).reshape(-1, *groups[0].shape[1:])


def gate_up(w):
    u = unit_tiles(w)
    return interleave(u[:FC], u[FC:])


def down(w):
    u = w.reshape(2, HALF, P, DC, P).transpose(3, 0, 2, 1, 4)
    return u.reshape(2 * DC, P, W11)


def columns(v):
    return v.reshape(-1, P).T


def padded(v):
    out = np.zeros((P, v.shape[1]), v.dtype)
    out[:v.shape[0]] = v
    return out


def constants():
    c = np.zeros((P, N_CONSTS), np.float32)

    def put(name, value):
        a, n = CONSTS[name]
        c[:value.shape[0], a:a + n] = value
    put("ident", np.eye(P, dtype=np.float32))
    swap = np.zeros((P, P), np.float32)
    cos, sin = np.ones((P, T), np.float32), np.zeros((P, T), np.float32)
    inv = np.float32(500000.0) ** (-np.arange(0, 16, 2, dtype=np.float32) / np.float32(16))
    ang = np.arange(T, dtype=np.float32)[None, :] * inv[:, None].astype(np.float32)
    for s in range(2):
        for i in range(8):
            a, b = 64 * s + i, 64 * s + 8 + i
            swap[b, a], swap[a, b] = -1.0, 1.0
            cos[a], cos[b] = np.cos(ang[i]), np.cos(ang[i])
            sin[a], sin[b] = np.sin(ang[i]), np.sin(ang[i])
    put("ropeswap", swap)
    put("cos", cos)
    put("sin", sin)
    put("causal", np.where(np.arange(P)[None, :] <= np.arange(P)[:, None], 0.0, NEG).astype(np.float32))
    put("ones64", (np.arange(P)[:, None] // 64 == np.arange(P)[None, :] // 64).astype(np.float32))
    put("pick", np.eye(16, dtype=np.float32))
    w = 2 << np.arange(4)
    put("invcount", np.tile((1.0 / np.minimum(np.arange(16)[None, :] + 1, w[:, None])).reshape(1, 64), (P, 1)).astype(np.float32))
    m = np.zeros((P, LEVELS, 64), np.int32)
    for i in range(LEVELS):
        b = 1 << i
        t = np.array([2 * b * n + b + r for n in range(64 // b) for r in range(b)])
        s = np.arange(P)
        m[:, i] = (s[:, None] // (2 * b) == t[None, :] // (2 * b)) & (s[:, None] % (2 * b) < b)
    return c, m


def layout(i):
    w8 = [gate_up(i["ffn1_w_gu"][0])]
    u = unit_tiles(i["conv_w_in"][0])
    w8 += [u[8:24], u[0:8], unit_tiles(i["conv_w_out"][0]), gate_up(i["ffn2_w_gu"][0]), gate_up(i["ffn1_w_gu"][1]),
           unit_tiles(i["attn_w_qkv"][0]), unit_tiles(i["attn_w_o"][0]), gate_up(i["ffn2_w_gu"][1]),
           unit_tiles(i["even_w_in_2"][0]), unit_tiles(i["even_w_out_2"][0]),
           unit_tiles(i["odd_w_in_2"][0][:, :4 * D]), unit_tiles(i["odd_w_out_2"][0])]
    w11 = [down(i["ffn1_w_down"][0]), down(i["ffn2_w_down"][0]), down(i["ffn1_w_down"][1]), down(i["ffn2_w_down"][1])]
    ada = np.concatenate([unit_tiles(i["ada_w_2"][l]) for l in range(2)]).reshape(48, P, DC, P)
    p = {
        "ln_ffn1": columns(i["ln_ffn1"].reshape(-1)), "ln_mix": columns(i["ln_mix"].reshape(-1)),
        "ln_ffn2": columns(i["ln_ffn2"].reshape(-1)), "conv_w": columns(i["conv_w"].reshape(-1)),
        "subln_g": columns(i["attn_subln_g"].reshape(-1)), "lam": padded(i["attn_lambda"][0].T),
        "c": columns(i["c_2"].reshape(-1)), "norm_g": columns(i["norm_g_2"].reshape(-1)),
        "ada_b": columns(i["ada_b_2"].reshape(-1)), "hgrn_lb": columns(i["hgrn_lb_2"].reshape(-1)),
        "onorm_g": columns(i["hgrn_onorm_g_2"].reshape(-1)), "pool_scale": columns(i["pool_scale_2"].reshape(-1)),
        "qnorm_g": np.tile(i["fox_qnorm_g_2"][0], 2)[:, None], "knorm_g": np.tile(i["fox_knorm_g_2"][0], 2)[:, None],
        "b_f": padded(i["fox_b_f_2"].T),
    }
    c, m = constants()
    x = np.concatenate([i["meta_tokens"], i["x"][0]]).T.reshape(DC, P, T).transpose(1, 0, 2)
    return {
        "w8": np.concatenate(w8), "w11": np.concatenate(w11), "ada_w": ada,
        "params": np.concatenate([p[n] for n in PARAMS], axis=1), "consts": c, "level_masks": m,
        "pool_w": i["pool_w_2"][0].transpose(1, 0, 2),
        "fl_w": i["odd_w_in_2"][0][:, 4 * D:].reshape(DC, P, 16).transpose(1, 0, 2),
        "x_in": x,
    }


def kernel(**inputs):
    import concourse.bacc as bacc
    from concourse.bass_utils import run_bass_kernel_spmd

    nc = bacc.Bacc("TRN2", target_bir_lowering=False, num_devices=1)
    arrays = {n: np.ascontiguousarray(a) for n, a in layout({n: np.asarray(a) for n, a in inputs.items()}).items()}
    args = [nc.dram_tensor(n, a.shape, mybir.dt.from_np(a.dtype), kind="ExternalInput").ap() for n, a in arrays.items()]
    out = nc.dram_tensor("out", (P, DC, SEQ), F32, kind="ExternalOutput").ap()
    build(nc, *args, out)
    r = run_bass_kernel_spmd(nc, [arrays], core_ids=[0])
    got = r.results[0]["out"]
    return np.ascontiguousarray(got.transpose(1, 0, 2).reshape(1, D, SEQ).transpose(0, 2, 1))
```
